# Optimizing a Trainium2 kernel written in Bass

```python
import math
import jax, jax.numpy as jnp
from jax import lax
import numpy as np

D_MODEL = 1024
BATCH = 1
SEQ = 2048
DEPTH = 1

PLE_DIM = 256
HG_HEADS = 8
HG_KEY = 128
HG_VAL = 128
HG_KWIDTH = HG_HEADS * HG_KEY
HG_WIDTH = HG_HEADS * HG_VAL
HG_CHUNK = 64
S5_GROUP = 16
S5_WIDTH = 512
S5_GROUPS = S5_WIDTH // S5_GROUP
S5_STATE = 64
DT_MIN = 0.001
DT_MAX = 0.1
NORM_EPS = 1e-6
IN_SIZES = (HG_KWIDTH, HG_KWIDTH, HG_WIDTH, HG_WIDTH, S5_WIDTH, S5_WIDTH, D_MODEL, D_MODEL)
IN_COLS = HG_KWIDTH * 2 + HG_WIDTH * 2 + S5_WIDTH * 2 + D_MODEL * 2

kernel_name = "hybrid_hgrn2_s5_gated_block"

def _split_points():
    pts, acc = [], 0
    for s in IN_SIZES[:-1]:
        acc += s
        pts.append(acc)
    return pts

def rms_norm(x, g):
    xf = x.astype(jnp.float32)
    y = xf * lax.rsqrt(jnp.mean(xf * xf, axis=-1, keepdims=True) + NORM_EPS)
    return (y * g.astype(jnp.float32)).astype(x.dtype)

def hgrn2_mix(q, f_logit, iv, lb):
    f32 = jnp.float32
    bsz, seq = q.shape[0], q.shape[1]
    nc = seq // HG_CHUNK
    lb = lb.reshape(HG_HEADS, HG_KEY).astype(f32)
    sig = jax.nn.sigmoid(f_logit.astype(f32))
    log_f = jnp.log(lb + (1.0 - lb) * sig)
    k = (1.0 - lb) * (1.0 - sig)
    chunk = lambda t: t.astype(f32).reshape(bsz, nc, HG_CHUNK, HG_HEADS, t.shape[-1])
    q, k, iv, log_f = chunk(q), chunk(k), chunk(iv), chunk(log_f)
    b = jnp.cumsum(log_f, axis=2)
    b_mid = b[:, :, HG_CHUNK // 2 - 1:HG_CHUNK // 2]
    b_last = b[:, :, HG_CHUNK - 1:HG_CHUNK]
    scores = jnp.einsum('bnthk,bnshk->bnhts', q * jnp.exp(b - b_mid), k * jnp.exp(b_mid - b))
    causal = jnp.tril(jnp.ones((HG_CHUNK, HG_CHUNK), dtype=bool))
    scores = jnp.where(causal, scores, 0.0)
    o_intra = jnp.einsum('bnhts,bnshv->bnthv', scores, iv)
    q_dec = q * jnp.exp(b)
    k_dec = k * jnp.exp(b_last - b)
    chunk_decay = jnp.exp(b_last[:, :, 0])

    def step(state, xs):
        qc, kc, ic, dc = xs
        o = jnp.einsum('bthk,bhkv->bthv', qc, state)
        state = dc[..., None] * state + jnp.einsum('bthk,bthv->bhkv', kc, ic)
        return state, o

    s0 = jnp.zeros((bsz, HG_HEADS, HG_KEY, HG_VAL), f32)
    mv = lambda t: jnp.moveaxis(t, 1, 0)
    _, o_inter = lax.scan(step, s0, (mv(q_dec), mv(k_dec), mv(iv), mv(chunk_decay)))
    o = o_intra + jnp.moveaxis(o_inter, 0, 1)
    return o.reshape(bsz, seq, HG_HEADS, HG_VAL)

def _cmul_combine(e1, e2):
    a1r, a1i, x1r, x1i = e1
    a2r, a2i, x2r, x2i = e2
    return (a1r * a2r - a1i * a2i,
            a1r * a2i + a1i * a2r,
            a2r * x1r - a2i * x1i + x2r,
            a2r * x1i + a2i * x1r + x2i)

def s5_mix(u, a_re, a_im, log_dt, b_re, b_im, c_re, c_im, d):
    f32 = jnp.float32
    uf = u.astype(f32)
    seq = u.shape[1]
    dt = jnp.exp(log_dt.astype(f32))[:, None]
    ar, ai = a_re.astype(f32), a_im.astype(f32)
    mag = jnp.exp(ar * dt)
    lr, li = mag * jnp.cos(ai * dt), mag * jnp.sin(ai * dt)
    den = ar * ar + ai * ai
    nr = lr - 1.0
    sr = (nr * ar + li * ai) / den
    si = (li * ar - nr * ai) / den
    br, bi = b_re.astype(f32), b_im.astype(f32)
    bbr = sr[..., None] * br - si[..., None] * bi
    bbi = sr[..., None] * bi + si[..., None] * br
    xr = jnp.einsum('bsgc,gnc->bsgn', uf, bbr)
    xi = jnp.einsum('bsgc,gnc->bsgn', uf, bbi)
    shape = (1, seq) + lr.shape
    lam_r = jnp.broadcast_to(lr[None, None], shape)
    lam_i = jnp.broadcast_to(li[None, None], shape)
    _, _, hr, hi = lax.associative_scan(_cmul_combine, (lam_r, lam_i, xr, xi), axis=1)
    y = (jnp.einsum('bsgn,gcn->bsgc', hr, c_re.astype(f32))
         - jnp.einsum('bsgn,gcn->bsgc', hi, c_im.astype(f32))
         + d.astype(f32) * uf)
    return y

def setup_inputs(seed: int = 0) -> dict:
    key = jax.random.key(seed)
    ks = jax.random.split(key, 24)
    n = lambda k, shape, scale: jax.random.normal(k, shape, jnp.float32) * scale
    L, G, N, C = DEPTH, S5_GROUPS, S5_STATE, S5_GROUP
    a_im_base = jnp.pi * jnp.arange(N, dtype=jnp.float32)
    return {
        "x": n(ks[0], (BATCH, SEQ, D_MODEL), 1.0),
        "p": n(ks[1], (DEPTH, BATCH, SEQ, PLE_DIM), 1.0),
        "norm_g": 1.0 + n(ks[2], (L, D_MODEL), 0.02),
        "w_in": n(ks[3], (L, D_MODEL, IN_COLS), D_MODEL ** -0.5),
        "hg_lb": n(ks[4], (DEPTH + 1, HG_KWIDTH), 0.1),
        "hg_norm_g": 1.0 + n(ks[5], (L, HG_WIDTH), 0.02),
        "w_o_hg": n(ks[6], (L, HG_WIDTH, D_MODEL), HG_WIDTH ** -0.5),
        "s5_a_re": -0.5 + n(ks[7], (L, G, N), 0.01),
        "s5_a_im": a_im_base[None, None, :] + n(ks[8], (L, G, N), 0.01),
        "s5_log_dt": jax.random.uniform(ks[9], (L, G), jnp.float32, math.log(DT_MIN), math.log(DT_MAX)),
        "s5_b_re": n(ks[10], (L, G, N, C), (2.0 * C) ** -0.5),
        "s5_b_im": n(ks[11], (L, G, N, C), (2.0 * C) ** -0.5),
        "s5_c_re": n(ks[12], (L, G, C, N), N ** -0.5),
        "s5_c_im": n(ks[13], (L, G, C, N), N ** -0.5),
        "s5_d": n(ks[14], (L, G, C), 1.0),
        "w_glu": n(ks[15], (L, S5_WIDTH, 2 * S5_WIDTH), S5_WIDTH ** -0.5),
        "b_glu": n(ks[16], (L, 2 * S5_WIDTH), 0.01),
        "w_o_s5": n(ks[17], (L, S5_WIDTH, D_MODEL), S5_WIDTH ** -0.5),
        "w_out": n(ks[18], (L, D_MODEL, D_MODEL), D_MODEL ** -0.5),
        "ple_norm_g": 1.0 + n(ks[19], (L, D_MODEL), 0.02),
        "w_ple": n(ks[20], (L, PLE_DIM, D_MODEL), PLE_DIM ** -0.5),
        "w_ple_gate": n(ks[21], (L, D_MODEL, D_MODEL), D_MODEL ** -0.5),
        "final_norm_g": 1.0 + n(ks[22], (D_MODEL,), 0.02),
    }

def reference(x, p, norm_g, w_in, hg_lb, hg_norm_g, w_o_hg, s5_a_re, s5_a_im, s5_log_dt,
              s5_b_re, s5_b_im, s5_c_re, s5_c_im, s5_d, w_glu, b_glu, w_o_s5, w_out,
              ple_norm_g, w_ple, w_ple_gate, final_norm_g):
    bsz, seq = x.shape[0], x.shape[1]
    h = x
    lb_all = jnp.cumsum(jax.nn.softmax(hg_lb.astype(jnp.float32), axis=0), axis=0)
    for l in range(DEPTH):
        u = rms_norm(h, norm_g[l])
        proj = u @ w_in[l]
        q, f_logit, iv, g_hg, u_s, z_s, gate_hg, gate_s5 = jnp.split(proj, _split_points(), axis=-1)

        o = hgrn2_mix(q.reshape(bsz, seq, HG_HEADS, HG_KEY),
                      f_logit.reshape(bsz, seq, HG_HEADS, HG_KEY),
                      iv.reshape(bsz, seq, HG_HEADS, HG_VAL), lb_all[l])
        o = rms_norm(o, hg_norm_g[l].reshape(HG_HEADS, HG_VAL)).reshape(bsz, seq, HG_WIDTH)
        y_hg = ((o * jax.nn.silu(g_hg.astype(jnp.float32))).astype(h.dtype) @ w_o_hg[l]).astype(h.dtype)

        ys = s5_mix(u_s.reshape(bsz, seq, S5_GROUPS, S5_GROUP), s5_a_re[l], s5_a_im[l], s5_log_dt[l],
                    s5_b_re[l], s5_b_im[l], s5_c_re[l], s5_c_im[l], s5_d[l]).reshape(bsz, seq, S5_WIDTH)
        ys = jax.nn.gelu(ys).astype(h.dtype)
        glu_a, glu_b = jnp.split(ys @ w_glu[l] + b_glu[l], 2, axis=-1)
        ys = glu_a * jax.nn.sigmoid(glu_b) * jax.nn.silu(z_s)
        y_s5 = (ys @ w_o_s5[l]).astype(h.dtype)

        merged = jax.nn.sigmoid(gate_hg) * y_hg + jax.nn.sigmoid(gate_s5) * y_s5
        h = h + (merged @ w_out[l]).astype(h.dtype)

        pe = p[l] @ w_ple[l]
        gate = jax.nn.sigmoid(rms_norm(h, ple_norm_g[l]) @ w_ple_gate[l])
        h = h + (pe * gate).astype(h.dtype)
    return rms_norm(h, final_norm_g)


_drawn_inputs = setup_inputs


def setup_inputs(seed=0):
    import zlib

    import numpy as np

    out = dict(_drawn_inputs(seed))
    spreads = {}
    factors = {'norm_g': 4.389,
     'hg_norm_g': 60.724,
     's5_a_re': 64.0,
     's5_a_im': 52.616,
     's5_log_dt': 53.472,
     's5_b_re': 64.0,
     's5_b_im': 64.0,
     's5_c_re': 64.0,
     's5_c_im': 64.0,
     'b_glu': 168.24,
     'ple_norm_g': 200.0,
     'final_norm_g': 22.472,
     'p': 3.542,
     'w_ple': 3.544,
     'w_ple_gate': 5.042}
    for name, (base, spread) in spreads.items():
        noise = np.random.default_rng([zlib.crc32(name.encode()), seed]).standard_normal(out[name].shape)
        drawn = base * np.exp(spread * noise) if base else spread * noise
        out[name] = __import__('jax').numpy.asarray(drawn.astype(out[name].dtype))
    for name, factor in factors.items():
        out[name] = (out[name] * factor).astype(out[name].dtype)
    return out
```

```python
from contextlib import ExitStack

import concourse.bass as bass
from concourse import mybir

F32 = mybir.dt.float32
F32R = mybir.dt.float32r
U32 = mybir.dt.uint32
ALU = mybir.AluOpType
ACT = mybir.ActivationFunctionType
ds = bass.ds

P = 128
SEQ = 2048
D = 1024
KT = D // P
TT = 512
NT = SEQ // TT
HEADS = 8
CH = 64
NCH = TT // CH
NPAIR = TT // P
EPS = 1e-6
S5W = 512
S5KT = S5W // P
PLE = 256
PLEKT = PLE // P
GRP = 32
GC = 16
NS = 64
SC = 8
NCK = SEQ // SC
PAIRS = GRP // 2
TWO_PI = 6.283185
MAGIC = 12582912.0
QB, FB, IB, GB = 0, 8, 16, 24
UB, ZB, HB, SB = 32, 36, 40, 48


class Bufs:

    keep = None

    def __init__(self, nc, tag):
        self.nc, self.tag, self.stack, self.nums = nc, tag, ExitStack(), []

    def __enter__(self):
        self.stack.__enter__()
        return self

    def __exit__(self, *a):
        return self.stack.__exit__(*a)

    def sb(self, name, shape, dt=F32):
        return self.stack.enter_context(self.nc.sbuf_tensor(f"{self.tag}_{name}", shape, dt))

    def ps(self, name, shape=(P, TT)):
        return self.stack.enter_context(self.nc.psum_tensor(f"{self.tag}_{name}", list(shape), F32))

    def sem(self, name):
        s = self.stack.enter_context(self.nc.semaphore(f"{self.tag}_{name}"))
        self.nums.append(s.num)
        return s

    def pool_dma_sem(self, name):
        return self.keep.enter_context(self.nc.semaphore(f"{self.tag}_{name}"))

    def clear(self):
        nums = sorted(self.nums)
        starts = [n for n in nums if n - 1 not in nums]
        ends = [n for n in nums if n + 1 not in nums]
        for lo, hi in zip(starts, ends):
            self.nc.gpsimd.sem_clear(range(lo, hi + 1))
        self.nc.all_engine_barrier()

    def block(self):
        self.stack.callback(self.clear)
        return self.stack.enter_context(self.nc.Block())


def split_matmuls(pe, out, w_hi, w_lo, u_hi, u_lo, first, last):
    pe.matmul(out, w_hi, u_hi, start=first, stop=False)
    pe.matmul(out, w_hi, u_lo, start=False, stop=False)
    return pe.matmul(out, w_lo, u_hi, start=False, stop=last)


def phase_norm_in(nc, c, a, u_hi, u_lo):
    with Bufs(nc, "n0") as m:
        xs = m.sb("xs", [P, 2, KT, TT])
        sq = m.sb("sq", [P, 2, TT])
        rstd = m.sb("rstd", [P, TT])
        u = m.sb("u", [P, 2, TT])
        lb2 = m.sb("lb2", [P, 2, HEADS])
        lbm = m.sb("lbm", [P, HEADS])
        lbs = m.sb("lbs", [P, HEADS])
        ms = m.ps("ms", (P, NT, TT))
        x_in = [m.sem(f"x_in{i}") for i in range(2)]
        small_in = m.sem("small_in")
        sq_done, ms_done, ln_done, rstd_done = (m.sem(n) for n in ("sq", "ms", "ln", "rstd"))
        u_done, hi_done, lo_done = (m.sem(n) for n in ("u", "hi", "lo"))
        ones_done, lb_done, lbe_done = m.sem("ones"), m.sem("lb"), m.sem("lbe")
        mk = m.sem("masks")
        block = m.block()

        @block.sync
        def _(sp):
            for dst, src in ((c["norm_g"][:], a["norm_g"]), (c["ple_g"][:], a["ple_norm_g"]),
                             (c["fin_g"][:], a["final_norm_g"]), (c["hg_g"][:], a["hg_norm_g"]),
                             (c["b_glu"][:], a["b_glu"]), (lb2[:], a["hg_lb"])):
                sp.dma_start(dst, src).then_inc(small_in, 16)
            for t in range(NT):
                if t >= 2:
                    sp.wait_ge(u_done, KT * (t - 1))
                sp.dma_start(xs[:, t % 2], a["x"][:, :, t * TT:(t + 1) * TT]).then_inc(x_in[t % 2], 16)

        @block.gpsimd
        def _(pool):
            pool.memset(c["ones"][:], 1.0).then_inc(ones_done, 1)
            pool.memset(c["ident"][:], 0.0).then_inc(mk, 1)
            pool.memset(c["causal"][:], 1.0).then_inc(mk, 1)
            pool.memset(c["restart"][:], 1.0).then_inc(mk, 1)
            pool.wait_ge(mk, 3)
            pool.affine_select(out=c["ident"][:], in_=c["ident"][:], compare_op=ALU.not_equal, fill=1.0,
                               base=0, pattern=[[-1, P]], channel_multiplier=1).then_inc(mk, 1)
            pool.affine_select(out=c["causal"][:], in_=c["causal"][:], compare_op=ALU.is_ge, fill=0.0,
                               base=0, pattern=[[1, P]], channel_multiplier=-1).then_inc(mk, 1)
            pool.memset(c["restart"][:].rearrange("p (n j) -> p n j", j=CH)[:, :, 0:1], 0.0).then_inc(mk, 1)
            pool.wait_ge(mk, 5)
            pool.memset(c["causal"][0:CH, CH:P], 0.0).then_inc(mk, 1)

        @block.tensor
        def _(pe):
            pe.wait_ge(ones_done, 1)
            for t in range(NT):
                for k in range(KT):
                    pe.wait_ge(sq_done, t * KT + k + 1)
                    pe.matmul(ms[:, t], c["ones"][:], sq[:, k % 2], start=k == 0, stop=k == KT - 1).then_inc(ms_done, 1)

        @block.scalar
        def _(act):
            for t in range(NT):
                act.wait_ge(x_in[t % 2], 16 * (t // 2 + 1))
                for k in range(KT):
                    n = t * KT + k
                    if n >= 2:
                        act.wait_ge(ms_done, n - 1)
                    act.activation(sq[:, k % 2], xs[:, t % 2, k], ACT.Square).then_inc(sq_done, 1)
                act.wait_ge(ms_done, KT * (t + 1))
                if t == 0:
                    act.preload_act_table_set("natural_log_exp_and_others")
                    act.wait_ge(lb_done, 1)
                if t >= 1:
                    act.wait_ge(u_done, KT * t)
                act.activation(rstd[:], ms[:, t], ACT.Ln, scale=1.0 / D, bias=c["eps"][:]).then_inc(ln_done, 1)
                act.wait_ge(ln_done, t + 1)
                act.activation(rstd[:], rstd[:], ACT.Exp, scale=-0.5).then_inc(rstd_done, 1)
                for k in range(KT):
                    act.wait_ge(u_done, t * KT + k + 1)
                    act.activation(u_hi[:, k, t * TT:(t + 1) * TT], u[:, k % 2], ACT.Copy).then_inc(hi_done, 1)
            act.wait_ge(lb_done, 3)
            act.activation(lb2[:], lb2[:], ACT.Exp).then_inc(lbe_done, 1)

        @block.vector
        def _(dve):
            def split_lo(n):
                t, k = n // KT, n % KT
                dve.wait_ge(hi_done, n + 1)
                at = slice(t * TT, (t + 1) * TT)
                dve.tensor_tensor(u_lo[:, k, at], u[:, k % 2], u_hi[:, k, at].bitcast(F32), ALU.subtract).then_inc(lo_done, 1)

            dve.memset(c["eps"][:], EPS).then_inc(lb_done, 1)
            dve.wait_ge(small_in, 16 * 6)
            dve.tensor_tensor(lbm[:], lb2[:, 0], lb2[:, 1], ALU.max).then_inc(lb_done, 1)
            dve.wait_ge(lb_done, 2)
            dve.tensor_tensor(lb2[:], lb2[:], lbm[:].rearrange("p (a h) -> p a h", a=1).to_broadcast([P, 2, HEADS]),
                              ALU.subtract).then_inc(lb_done, 1)
            for t in range(NT):
                dve.wait_ge(rstd_done, t + 1)
                for k in range(KT):
                    n = t * KT + k
                    if n >= 2:
                        dve.wait_ge(hi_done, n - 1)
                        dve.wait_ge(lo_done, n - 1)
                    dve.scalar_tensor_tensor(u[:, k % 2], xs[:, t % 2, k], c["norm_g"][:, k:k + 1], rstd[:],
                                             ALU.mult, ALU.mult).then_inc(u_done, 1)
                    if n >= 1:
                        split_lo(n - 1)
            split_lo(NT * KT - 1)
            dve.wait_ge(lbe_done, 1)
            dve.tensor_tensor(lbs[:], lb2[:, 0], lb2[:, 1], ALU.add).then_inc(lb_done, 1)
            dve.wait_ge(lb_done, 4)
            dve.reciprocal(lbs[:], lbs[:]).then_inc(lb_done, 1)
            dve.wait_ge(lb_done, 5)
            dve.tensor_tensor(c["lb"][:], lb2[:, 0], lbs[:], ALU.mult).then_inc(lb_done, 1)
            dve.wait_ge(lb_done, 6)
            dve.tensor_scalar(c["omlb"][:], c["lb"][:], -1.0, 1.0, ALU.mult, ALU.add).then_inc(lb_done, 1)
            dve.tensor_scalar(c["nomlb"][:], c["lb"][:], 1.0, None, ALU.subtract).then_inc(lb_done, 1)


def phase_hgrn(nc, c, a, u_hi, u_lo):
    STEPS = HEADS * NT
    KIND = [FB, GB, IB, QB]
    with Bufs(nc, "hg") as m:
        raw = m.sb("raw", [P, 2, KT, P])
        w_hi = m.sb("w_hi", [P, 4, KT, P], F32R)
        w_lo = m.sb("w_lo", [P, 4, KT, P], F32R)
        sig = m.sb("sig", [P, TT])
        lf = m.sb("lf", [P, TT])
        b = m.sb("b", [P, TT])
        qe = m.sb("qe", [P, TT])
        ke = m.sb("ke", [P, TT])
        iv = m.sb("iv", [P, TT])
        sg = m.sb("sg", [P, 2, TT])
        ken = m.sb("ken", [P, NPAIR, P])
        ivn = m.sb("ivn", [P, NPAIR, P])
        sT = m.sb("sT", [P, NPAIR, P])
        osq = m.sb("osq", [P, TT])
        y = m.sb("y", [P, TT])
        S = m.sb("S", [P, NCH, P])
        G = m.sb("G", [P, P])
        R = m.sb("R", [P, NCH + 1])
        coef = m.sb("coef", [P, NCH])
        pf, pg, pi, pq = (m.ps(n) for n in ("pf", "pg", "pi", "pq"))
        pk, pv, psc, po = (m.ps(n) for n in ("pk", "pv", "psc", "po"))
        raw_in = [m.sem(f"raw_in{i}") for i in range(2)]
        w_hi_done, w_lo_done, proj_done = m.sem("w_hi"), m.sem("w_lo"), m.sem("proj")
        turned, kv_done, o_done, ms_done = (m.sem(n) for n in ("turned", "kv", "o", "ms"))
        sigf, sigg, iv_done, lf_done = (m.sem(n) for n in ("sigf", "sigg", "ivc", "lfd"))
        coef_done, e2_done, e1_done = m.sem("coefd"), m.sem("e2"), m.sem("e1")
        ivn_done, osq_done, ln_done, rstd_done = (m.sem(n) for n in ("ivn", "osqd", "ln", "rstdd"))
        ken_done, masked, states, sg_done = (m.sem(n) for n in ("kend", "masked", "states", "sgd"))
        lfin_done, scan_done, arg_done, d_done = (m.sem(n) for n in ("lfin", "scan", "arg", "d"))
        ke_done, qe_done, yn_done, y_done = (m.sem(n) for n in ("ked", "qed", "yn", "yd"))
        r_done, g_done = m.sem("r"), m.sem("g")
        zeroed, o_out = m.sem("zeroed"), m.pool_dma_sem("o_out")
        block = m.block()

        def heads(engine, head):
            head(0, True, False)
            with engine.Fori(1, HEADS - 1) as h:
                head(h, False, False)
            head(HEADS - 1, False, True)

        @block.sync
        def _(sp):
            def head(h, first, last):
                for kind in range(4):
                    if not first or kind >= 2:
                        sp.wait_ge(w_lo_done, h * 4 + kind - 1)
                    sp.dma_start(raw[:, kind % 2], a["w_in"][ds(h + KIND[kind], 1)].rearrange("a p k c -> (a p) k c")
                                 ).then_inc(raw_in[kind % 2], 16)
            heads(sp, head)

        @block.gpsimd
        def _(pool):
            def head(h, first, last):
                for t in range(NT):
                    pool.wait_ge(y_done, h * NT + t + 1)
                    pool.dma_start(a["o_gated"][ds(h, 1), :, t * TT:(t + 1) * TT].rearrange("a p n -> (a p) n"),
                                   y[:]).then_inc(o_out, 16)
            pool.memset(sT[:], 0.0).then_inc(zeroed, 1)
            heads(pool, head)
            pool.wait_ge(o_out, 16 * STEPS)

        @block.tensor
        def _(pe):
            def project(n, t, kind, new_weights):
                if new_weights:
                    pe.wait_ge(w_lo_done, n + kind + 1)
                out = (pf, pg, pi, pq)[kind]
                at = slice(t * TT, (t + 1) * TT)
                for k in range(KT):
                    ins = split_matmuls(pe, out[:], w_hi[:, kind, k], w_lo[:, kind, k], u_hi[:, k, at], u_lo[:, k, at],
                                        k == 0, k == KT - 1)
                ins.then_inc(proj_done, 1)

            def turn(s, first):
                pe.wait_ge(ke_done, s + 1)
                if not first:
                    pe.wait_ge(g_done, s * NCH)
                for p in range(NPAIR):
                    at = slice(p * P, (p + 1) * P)
                    pe.transpose(pk[:, at], ke[:, at], c["ident"][:]).then_inc(turned, 1)
                pe.wait_ge(iv_done, s + 1)
                for p in range(NPAIR):
                    at = slice(p * P, (p + 1) * P)
                    pe.transpose(pv[:, at], iv[:, at], c["ident"][:]).then_inc(turned, 1)
                pe.wait_ge(qe_done, s + 1)
                if not first:
                    pe.wait_ge(ln_done, s)
                for p in range(NPAIR):
                    at = slice(p * P, (p + 1) * P)
                    pe.matmul(psc[:, at], ke[:, at], qe[:, at], start=True, stop=True).then_inc(turned, 1)

            def outer(s):
                pe.wait_ge(ken_done, s + 1)
                pe.wait_ge(ivn_done, s + 1)
                for j in range(NCH):
                    rows = slice(j % 2 * CH, j % 2 * CH + CH)
                    out = (pk, pv)[j % 2][:, j // 2 * P:j // 2 * P + P]
                    ins = pe.matmul(out, ken[rows, j // 2], ivn[rows, j // 2], start=True, stop=True)
                ins.then_inc(kv_done, 1)

            def attend(s, first):
                pe.wait_ge(masked, s + 1)
                if not first:
                    pe.wait_ge(yn_done, s)
                for p in range(NPAIR):
                    for j in (2 * p, 2 * p + 1):
                        pe.wait_ge(states, s * NCH + j + 1)
                        at = slice(j * CH, (j + 1) * CH)
                        pe.matmul(po[:, at], S[:, j], qe[:, at], start=j % 2 == 0, stop=False, skip_group_check=True)
                    pe.matmul(po[:, p * P:(p + 1) * P], ivn[:, p], sT[:, p], start=False, stop=True,
                              skip_group_check=True).then_inc(o_done, 1)

            def mean_square(s):
                pe.wait_ge(osq_done, s + 1)
                pe.matmul(psc[:], c["ones"][:], osq[:], start=True, stop=True).then_inc(ms_done, 1)

            def head(h, first, last):
                for t in range(NT):
                    n = h * NT + t
                    recur = not (first and t == 0)
                    if recur:
                        pe.wait_ge(sigf, n)
                    project(n, t, 0, t == 0)
                    if recur:
                        turn(n - 1, first and t == 1)
                        pe.wait_ge(sg_done, n)
                    project(n, t, 1, t == 0)
                    if recur:
                        outer(n - 1)
                    project(n, t, 2, t == 0)
                    if recur:
                        attend(n - 1, first and t == 1)
                    project(n, t, 3, t == 0)
                    if recur:
                        mean_square(n - 1)
            heads(pe, head)
            turn(STEPS - 1, False)
            outer(STEPS - 1)
            attend(STEPS - 1, False)
            mean_square(STEPS - 1)

        @block.scalar
        def _(act):
            def round_weights(h, kind):
                act.wait_ge(raw_in[kind % 2], (h * 2 + kind // 2 + 1) * 16)
                act.activation(w_hi[:, kind], raw[:, kind % 2], ACT.Copy).then_inc(w_hi_done, 1)

            def turned_iv(s):
                act.wait_ge(turned, s * 3 * NPAIR + 2 * NPAIR)
                act.activation(ivn[:].rearrange("p a n -> p (a n)"), pv[:], ACT.Copy).then_inc(ivn_done, 1)

            def norm(s, first):
                act.wait_ge(o_done, (s + 1) * NPAIR)
                if not first:
                    act.wait_ge(yn_done, s)
                act.activation(osq[:], po[:], ACT.Square).then_inc(osq_done, 1)
                act.wait_ge(ms_done, s + 1)
                act.activation(osq[:], psc[:], ACT.Ln, scale=1.0 / P, bias=c["eps"][:]).then_inc(ln_done, 1)
                act.wait_ge(ln_done, s + 1)
                act.activation(osq[:], osq[:], ACT.Exp, scale=-0.5).then_inc(rstd_done, 1)

            def head(h, first, last):
                for t in range(NT):
                    n = h * NT + t
                    recur = not (first and t == 0)
                    split = t == NT - 1 and not last
                    act.wait_ge(proj_done, n * 4 + 1)
                    if recur:
                        act.wait_ge(ke_done, n)
                    act.activation(sig[:], pf[:], ACT.Sigmoid).then_inc(sigf, 1)
                    if split:
                        round_weights(h + 1, 0)
                    if recur:
                        turned_iv(n - 1)
                    act.wait_ge(proj_done, n * 4 + 2)
                    if not first or t >= 2:
                        act.wait_ge(y_done, n - 1)
                    act.activation(sg[:, t % 2], pg[:], ACT.Sigmoid).then_inc(sigg, 1)
                    act.preload_act_table_set("natural_log_exp_and_others")
                    act.wait_ge(lfin_done, n + 1)
                    act.activation(lf[:], lf[:], ACT.Ln).then_inc(lf_done, 1)
                    if split:
                        round_weights(h + 1, 1)
                    act.wait_ge(arg_done, n + 1)
                    act.activation(coef[:], coef[:], ACT.Exp).then_inc(coef_done, 1)
                    act.wait_ge(d_done, n + 1)
                    act.activation(b[:], lf[:], ACT.Exp, scale=-1.0).then_inc(e2_done, 1)
                    act.activation(lf[:], lf[:], ACT.Exp).then_inc(e1_done, 1)
                    act.wait_ge(proj_done, n * 4 + 3)
                    act.activation(iv[:], pi[:], ACT.Copy).then_inc(iv_done, 1)
                    if split:
                        round_weights(h + 1, 2)
                    if recur:
                        norm(n - 1, first and t == 1)
                    if split:
                        act.wait_ge(proj_done, n * 4 + 4)
                        round_weights(h + 1, 3)

            for kind in range(4):
                round_weights(0, kind)
            heads(act, head)
            turned_iv(STEPS - 1)
            norm(STEPS - 1, False)

        @block.vector
        def _(dve):
            mids = b[:].rearrange("p (n j) -> p n j", j=CH)[:, :, CH // 2 - 1:CH // 2]
            ends = b[:].rearrange("p (n j) -> p n j", j=CH)[:, :, CH - 1:CH]
            chunks = lambda x: x[:].rearrange("p (n j) -> p n j", j=CH)
            col = lambda x: x.rearrange("p (n a) -> p n a", a=1)

            def split_weights(h, kind):
                dve.wait_ge(w_hi_done, h * 4 + kind + 1)
                dve.tensor_tensor(w_lo[:, kind], raw[:, kind % 2], w_hi[:, kind].bitcast(F32),
                                  ALU.subtract).then_inc(w_lo_done, 1)

            def turned_scores(s):
                dve.wait_ge(turned, (s + 1) * 3 * NPAIR)
                dve.tensor_copy(ken[:].rearrange("p a n -> p (a n)"), pk[:]).then_inc(ken_done, 1)
                dve.copy_predicated(sT[:], c["causal"][:].rearrange("p (a n) -> p a n", a=1).to_broadcast([P, NPAIR, P]).bitcast(U32),
                                    psc[:].rearrange("p (a n) -> p a n", a=NPAIR)).then_inc(masked, 1)

            def carry_state(s, new_head):
                dve.wait_ge(kv_done, s + 1)
                for j in range(NCH):
                    kv = (pk, pv)[j % 2][:, j // 2 * P:j // 2 * P + P]
                    if new_head and j == 0:
                        dve.memset(S[:, 0], 0.0).then_inc(states, 1)
                        dve.wait_ge(states, s * NCH + 1)
                        dve.tensor_copy(G[:], kv).then_inc(g_done, 1)
                        continue
                    if j == 0:
                        dve.wait_ge(coef_done, s + 1)
                    dve.wait_ge(g_done, s * NCH + j)
                    dve.tensor_scalar(S[:, j], G[:], coef[:, j:j + 1], None, ALU.mult).then_inc(states, 1)
                    dve.wait_ge(states, s * NCH + j + 1)
                    dve.tensor_tensor(G[:], kv, S[:, j], ALU.add).then_inc(g_done, 1)

            def gate(s, h, t):
                dve.wait_ge(rstd_done, s + 1)
                if not (isinstance(s, int) and s == 0):
                    dve.wait_ge(o_out, s * 16)
                dve.scalar_tensor_tensor(y[:], po[:], c["hg_g"][:, ds(h, 1)], osq[:], ALU.mult, ALU.mult).then_inc(yn_done, 1)
                dve.wait_ge(yn_done, s + 1)
                dve.tensor_tensor(y[:], y[:], sg[:, t % 2], ALU.mult).then_inc(y_done, 1)

            def head(h, first, last):
                for t in range(NT):
                    n = h * NT + t
                    recur = not (first and t == 0)
                    split = t == NT - 1 and not last
                    if recur:
                        dve.wait_ge(qe_done, n)
                    dve.wait_ge(sigf, n + 1)
                    dve.tensor_scalar(lf[:], sig[:], c["omlb"][:, ds(h, 1)], c["lb"][:, ds(h, 1)], ALU.mult,
                                      ALU.add).then_inc(lfin_done, 1)
                    if split:
                        split_weights(h + 1, 0)
                    if recur:
                        turned_scores(n - 1)
                        carry_state(n - 1, t == 1)
                    dve.wait_ge(sigg, n + 1)
                    dve.tensor_tensor(sg[:, t % 2], pg[:], sg[:, t % 2], ALU.mult).then_inc(sg_done, 1)
                    dve.wait_ge(lf_done, n + 1)
                    dve.tensor_tensor_scan(b[:], c["restart"][:], lf[:], 0.0, ALU.mult, ALU.add).then_inc(scan_done, 1)
                    if split:
                        split_weights(h + 1, 1)
                    dve.wait_ge(scan_done, n + 1)
                    dve.wait_ge(r_done, 2 * n + 1)
                    dve.tensor_tensor(col(R[:, 1:NCH + 1]), ends, mids, ALU.subtract).then_inc(r_done, 1)
                    dve.wait_ge(r_done, 2 * n + 2)
                    dve.tensor_tensor(col(coef[:]), col(R[:, 0:NCH]), mids, ALU.add).then_inc(arg_done, 1)
                    dve.tensor_tensor(chunks(lf), chunks(b), mids.to_broadcast([P, NCH, CH]), ALU.subtract).then_inc(d_done, 1)
                    dve.wait_ge(arg_done, n + 1)
                    dve.tensor_copy(R[:, 0:1], R[:, NCH:NCH + 1]).then_inc(r_done, 1)
                    dve.wait_ge(e2_done, n + 1)
                    dve.scalar_tensor_tensor(ke[:], sig[:], 1.0, b[:], ALU.subtract, ALU.mult).then_inc(ke_done, 1)
                    if split:
                        split_weights(h + 1, 2)
                    dve.wait_ge(proj_done, n * 4 + 4)
                    dve.wait_ge(e1_done, n + 1)
                    dve.scalar_tensor_tensor(qe[:], pq[:], c["nomlb"][:, ds(h, 1)], lf[:], ALU.mult, ALU.mult).then_inc(qe_done, 1)
                    if recur:
                        gate(n - 1, h - 1 if t == 0 else h, (t - 1) % NT)
                    if split:
                        split_weights(h + 1, 3)

            for kind in range(4):
                split_weights(0, kind)
            dve.memset(R[:], 0.0).then_inc(r_done, 1)
            dve.wait_ge(zeroed, 1)
            heads(dve, head)
            turned_scores(STEPS - 1)
            carry_state(STEPS - 1, False)
            gate(STEPS - 1, HEADS - 1, NT - 1)


def phase_s5(nc, c, a, u_hi, u_lo):
    NB, U_BLOCKS, Z_BLOCKS = 24, S5KT, 2 * S5KT
    NL = 2 * SC + 1
    NW = NCK // NT
    with Bufs(nc, "s5") as m:
        raw = m.sb("raw", [P, 2, KT, P])
        w_hi = m.sb("w_hi", [P, 2, KT, P], F32R)
        w_lo = m.sb("w_lo", [P, 2, KT, P], F32R)
        stage = m.sb("stage", [P, NT, TT])
        are, aim, dt = m.sb("are", [P, PAIRS]), m.sb("aim", [P, PAIRS]), m.sb("dt", [P, PAIRS])
        bre, bim = m.sb("bre", [P, PAIRS, GC]), m.sb("bim", [P, PAIRS, GC])
        cre, cim = m.sb("cre", [P, PAIRS, GC]), m.sb("cim", [P, PAIRS, GC])
        dd = m.sb("dd", [GC, 2, PAIRS])
        kk = m.sb("kk", [P, NL])
        nn = m.sb("nn", [P, NCK])
        adt, turns = m.sb("adt", [P, PAIRS]), m.sb("turns", [P, PAIRS])
        mag, tn = m.sb("mag", [P, PAIRS, NL]), m.sb("tn", [P, PAIRS, NL])
        lr, li = m.sb("lr", [P, PAIRS, NL]), m.sb("li", [P, PAIRS, NL])
        den, nr = m.sb("den", [P, PAIRS]), m.sb("nr", [P, PAIRS])
        sr, si, st = m.sb("sr", [P, PAIRS]), m.sb("si", [P, PAIRS]), m.sb("st", [P, PAIRS])
        rho = m.sb("rho", [P, PAIRS])
        f_hi, f_lo = m.sb("f_hi", [P, PAIRS]), m.sb("f_lo", [P, PAIRS])
        bb = m.sb("bb", [P, 2, GC])
        X = m.sb("X", [P, 2, SC, GC])
        Z = m.sb("Z", [P, 2, SC + 1, GC])
        mt = m.sb("mt", [P, SC + 1, GC])
        w_in_t = m.sb("w_in_t", [P, 2, P])
        msb = m.sb("msb", [GC, 2, SC, GC])
        w_intra = m.sb("w_intra", [P, 2, 2, P])
        U = m.sb("U", [P, 2, 2, NCK])
        trig = m.sb("trig", [P, 2, NCK])
        t1, t2 = m.sb("t1", [P, NCK]), m.sb("t2", [P, NCK])
        xt = m.sb("xt", [P, 2, NCK])
        Hp = m.sb("Hp", [P, 2, NCK])
        ysb = m.sb("ysb", [P, 2, 2, NCK])
        ps = [m.ps(f"ps{t}") for t in range(NT)]
        py = [m.ps(f"py{q}") for q in range(2)]
        px, pin = m.ps("px"), m.ps("pin")
        raw_in = [m.sem(f"raw_in{i}") for i in range(2)]
        par_in, u_in = m.sem("par_in"), [m.sem(f"u_in{i}") for i in range(2)]
        w_hi_done, w_lo_done, proj_done = m.sem("w_hi_d"), m.sem("w_lo_d"), m.sem("proj")
        sig_done, staged, stored = m.sem("sig"), m.sem("staged"), m.pool_dma_sem("stored")
        consts_done, par_act, par_dve = m.sem("consts"), m.sem("par_act"), m.sem("par_dve")
        chain = m.sem("chain")
        mats_done, ang_done, trig_done = m.sem("mats"), m.sem("ang"), m.sem("trig_d")
        xz_done, turned_done, msb_done, intra_in = m.sem("xz"), m.sem("turned"), m.sem("msb_d"), m.sem("intra_in")
        pin_done, hp_done, y_done, gelu_done = m.sem("pin_d"), m.sem("hp_d"), m.sem("y_d"), m.sem("gelu_d")
        ys_out = [m.pool_dma_sem(f"ys_out{i}") for i in range(2)]
        zeroed = m.sem("zeroed")
        block = m.block()

        def slots(engine, body):
            for b in range(Z_BLOCKS):
                body(b, None, b % 2, b == 0, False)
            for p in range(2):
                body(Z_BLOCKS + p, p, p, p == 0, False)
            with engine.Fori(1, PAIRS // 2 - 1) as i:
                for r in range(2):
                    body(i * 2 + (Z_BLOCKS + r), i * 2 + r, r, False, False)
            for p in (PAIRS - 2, PAIRS - 1):
                body(Z_BLOCKS + p, p, p % 2, False, p == PAIRS - 1)

        @block.sync
        def _(sp):
            def load_weights(b, r):
                sp.dma_start(raw[:, r], a["w_in"][ds(b + UB, 1)].rearrange("a p k c -> (a p) k c")).then_inc(raw_in[r], 16)

            def load_u(p, r):
                for q in range(2):
                    src = a["us"][ds(p * 2 + q, 1)].rearrange("a c j n -> (a j) c n")
                    sp.dma_start(U[:, r, q], src).then_inc(u_in[r], 16)

            def body(b, p, r, first, last):
                if not (last or (p is not None and isinstance(p, int) and p == PAIRS - 2)):
                    sp.wait_ge(w_lo_done, b + 1)
                    load_weights(b + 2, r)
                if p is None:
                    if b == Z_BLOCKS - 1:
                        sp.wait_ge(stored, 16 * NT * U_BLOCKS)
                        load_u(0, 0)
                    return
                if not last:
                    if not first:
                        sp.wait_ge(y_done, p)
                    load_u(p + 1, 1 - r)
                sp.wait_ge(msb_done, p * 2 + 2)
                for j in range(SC):
                    rows = slice(j * GC, (j + 1) * GC)
                    sp.dma_start(w_intra[rows, r, :, j * GC:P], msb[:, :, 0:SC - j].rearrange("c q j d -> c q (j d)")
                                 ).then_inc(intra_in, 16)

            for dst, src in ((are[:], a["s5_a_re"]), (aim[:], a["s5_a_im"]), (bre[:], a["s5_b_re"]), (bim[:], a["s5_b_im"]),
                             (cre[:], a["s5_c_re"]), (cim[:], a["s5_c_im"]), (dd[:], a["s5_d"]),
                             (dt[0:NS], a["s5_log_dt"][0:1].to_broadcast([NS, PAIRS])),
                             (dt[NS:P], a["s5_log_dt"][1:2].to_broadcast([NS, PAIRS]))):
                sp.dma_start(dst, src).then_inc(par_in, 16)
            load_weights(0, 0)
            load_weights(1, 1)
            slots(sp, body)

        @block.gpsimd
        def _(pool):
            pool.iota(nn[:], pattern=[[1, NCK]], base=0, channel_multiplier=0,
                      allow_small_or_imprecise_dtypes=True).then_inc(consts_done, 1)
            pool.iota(kk[:, 0:SC + 1], pattern=[[1, SC + 1]], base=0, channel_multiplier=0,
                      allow_small_or_imprecise_dtypes=True).then_inc(consts_done, 1)
            pool.iota(kk[:, SC + 1:NL], pattern=[[-1, SC]], base=SC - 1, channel_multiplier=0,
                      allow_small_or_imprecise_dtypes=True).then_inc(consts_done, 1)
            pool.memset(w_intra[:], 0.0).then_inc(zeroed, 1)
            pool.memset(Hp[:], 0.0).then_inc(zeroed, 1)
            pool.wait_ge(zeroed, 2)

            def store_y(p, r):
                pool.wait_ge(gelu_done, p + 1)
                for q in range(2):
                    dst = a["ys"][ds(p * 2 + q, 1)].rearrange("a c j n -> (a j) c n")
                    pool.dma_start(dst, ysb[:, r, q]).then_inc(ys_out[r], 16)

            def body(b, p, r, first, last):
                if p is not None and not first:
                    store_y(p - 1, 1 - r)
                for t in range(NT):
                    pool.wait_ge(staged, b * NT + t + 1)
                    if p is None and b < U_BLOCKS:
                        dst = a["us"].rearrange("(k g) c j n -> k (g c) j n", k=S5KT)[b, :, :, t * NW:(t + 1) * NW]
                        src = stage[:, t].rearrange("p (j n) -> p j n", j=SC)
                    else:
                        out = a["silu_z"][b - U_BLOCKS:b - U_BLOCKS + 1] if p is None else a["gates"][ds(p, 1)]
                        dst = out[:, :, t * TT:(t + 1) * TT].rearrange("a p n -> (a p) n")
                        src = stage[:, t]
                    pool.dma_start(dst, src).then_inc(stored, 16)
                    pool.wait_ge(stored, (b * NT + t) * 16 + 16)
            slots(pool, body)
            store_y(PAIRS - 1, 1)
            for r in range(2):
                pool.wait_ge(ys_out[r], 16 * PAIRS)

        @block.tensor
        def _(pe):
            def project(b, r, t, first):
                if not first:
                    pe.wait_ge(staged, (b - 1) * NT + t + 1)
                at = slice(t * TT, (t + 1) * TT)
                for k in range(KT):
                    ins = split_matmuls(pe, ps[t][:], w_hi[:, r, k], w_lo[:, r, k], u_hi[:, k, at], u_lo[:, k, at],
                                        k == 0, k == KT - 1)
                ins.then_inc(proj_done, 1)

            def body(b, p, r, first, last):
                pe.wait_ge(w_lo_done, b + 1)
                project(b, r, 0, p is None and b == 0)
                if p is not None:
                    if not first:
                        pe.wait_ge(gelu_done, p)
                    pe.wait_ge(xz_done, p + 1)
                    for q in range(2):
                        pe.transpose(px[:, q * P:(q + 1) * P], X[:, q].rearrange("p j c -> p (j c)"), c["ident"][:])
                    for q in range(2):
                        rows = slice(q * NS, (q + 1) * NS)
                        for k in range(2):
                            ins = pe.matmul(py[q][0:GC, NCK:NCK + P], bb[rows, k],
                                            Z[rows, k, 0:SC].rearrange("p j c -> p (j c)"), start=k == 0, stop=k == 1)
                    ins.then_inc(mats_done, 1)
                project(b, r, 1, p is None and b == 0)
                if p is not None:
                    pe.wait_ge(turned_done, p + 1)
                    pe.wait_ge(u_in[r], (p // 2) * 32 + 32 if isinstance(p, int) else (p - r) * 16 + 32)
                    if not first:
                        pe.wait_ge(hp_done, p)
                    for k in range(2):
                        for q in range(2):
                            ins = pe.matmul(pin[q * NS:(q + 1) * NS, k * NCK:(k + 1) * NCK], w_in_t[:, k, q * NS:(q + 1) * NS],
                                            U[:, r, q], start=True, stop=True)
                    ins.then_inc(pin_done, 1)
                project(b, r, 2, p is None and b == 0)
                project(b, r, 3, p is None and b == 0)
                if p is not None:
                    pe.wait_ge(intra_in, (p + 1) * 16 * SC)
                    pe.wait_ge(hp_done, p + 1)
                    for q in range(2):
                        pe.matmul(py[q][:, 0:NCK], w_intra[:, r, q], U[:, r, q], start=True, stop=False)
                    for k in range(2):
                        for q in range(2):
                            rows = slice(q * NS, (q + 1) * NS)
                            ins = pe.matmul(py[q][:, 0:NCK], Z[rows, k, 1:SC + 1].rearrange("p j c -> p (j c)"),
                                            Hp[rows, k], start=False, stop=k == 1)
                    ins.then_inc(y_done, 1)
            slots(pe, body)

        @block.scalar
        def _(act):
            n_par = [0]

            def par(ins):
                n_par[0] += 1
                ins.then_inc(par_act, 1)

            def round_weights(b, r):
                act.wait_ge(raw_in[r], (b // 2) * 16 + 16 if isinstance(b, int) else b * 8 - r * 8 + 16)
                act.activation(w_hi[:, r], raw[:, r], ACT.Copy).then_inc(w_hi_done, 1)

            def gelu(p, r):
                act.wait_ge(y_done, p + 1)
                if not (isinstance(p, int) and p < 2):
                    act.wait_ge(ys_out[r], (p - r) * 16)
                for q in range(2):
                    ins = act.activation(ysb[:, r, q], py[q][:, 0:NCK], ACT.Gelu_apprx_tanh)
                ins.then_inc(gelu_done, 1)

            def body(b, p, r, first, last):
                if p is not None:
                    if not first:
                        gelu(p - 1, 1 - r)
                    act.wait_ge(ang_done, p + 1)
                    act.activation(trig[:], trig[:], ACT.Sin, scale=TWO_PI).then_inc(trig_done, 1)
                for t in range(NT):
                    act.wait_ge(proj_done, b * NT + t + 1)
                    if not (p is None and b == 0):
                        act.wait_ge(stored, ((b - 1) * NT + t) * 16 + 16)
                    if p is None and b < U_BLOCKS:
                        act.activation(stage[:, t].rearrange("p (j n) -> p j n", j=SC),
                                       ps[t][:].rearrange("p (n j) -> p j n", j=SC), ACT.Copy).then_inc(staged, 1)
                    elif p is None:
                        act.activation(stage[:, t], ps[t][:], ACT.Sigmoid).then_inc(sig_done, 1)
                    else:
                        act.activation(stage[:, t], ps[t][:], ACT.Sigmoid).then_inc(staged, 1)
                    if t == 0:
                        if not last:
                            round_weights(b + 1, 1 - r)
                        if p is not None:
                            act.wait_ge(mats_done, p + 1)
                            act.activation(w_in_t[:].rearrange("p k n -> p (k n)"), px[:, 0:2 * P], ACT.Copy).then_inc(turned_done, 1)

            round_weights(0, 0)
            act.wait_ge(par_in, 9 * 16)
            par(act.activation(dt[:], dt[:], ACT.Exp))
            act.wait_ge(par_dve, 4)
            par(act.activation(mag[:], mag[:], ACT.Exp))
            act.wait_ge(par_dve, 9)
            par(act.activation(li[:], li[:], ACT.Sin, scale=TWO_PI))
            par(act.activation(lr[:], lr[:], ACT.Sin, scale=TWO_PI))
            slots(act, body)
            gelu(PAIRS - 1, 1)

        @block.vector
        def _(dve):
            def split_weights(b, r):
                dve.wait_ge(w_hi_done, b + 1)
                dve.tensor_tensor(w_lo[:, r], raw[:, r], w_hi[:, r].bitcast(F32), ALU.subtract).then_inc(w_lo_done, 1)

            n_par = [0]

            def par(ins):
                n_par[0] += 1
                ins.then_inc(par_dve, 1)
                dve.wait_ge(par_dve, n_par[0])

            def parameters():
                bk = lambda x: x[:].rearrange("p (a b) -> p a b", b=1).to_broadcast([P, PAIRS, NL])
                bn = kk[:].rearrange("p (a b) -> p a b", a=1).to_broadcast([P, PAIRS, NL])
                at = lambda x, j: x[:, :, j:j + 1].rearrange("p a b -> p (a b)")
                dve.wait_ge(consts_done, 3)
                dve.wait_ge(par_act, 1)
                par(dve.tensor_tensor(adt[:], are[:], dt[:], ALU.mult))
                par(dve.scalar_tensor_tensor(turns[:], aim[:], 0.15915494309, dt[:], ALU.mult, ALU.mult))
                par(dve.tensor_tensor(tn[:], bk(turns), bn, ALU.mult))
                par(dve.tensor_tensor(mag[:], bk(adt), bn, ALU.mult))
                par(dve.tensor_scalar(li[:], tn[:], MAGIC, MAGIC, ALU.add, ALU.subtract))
                par(dve.tensor_tensor(tn[:], tn[:], li[:], ALU.subtract))
                par(dve.tensor_scalar(lr[:], tn[:], 0.25, None, ALU.add))
                par(dve.tensor_scalar(li[:], lr[:], MAGIC, MAGIC, ALU.add, ALU.subtract))
                dve.tensor_tensor(lr[:], lr[:], li[:], ALU.subtract).then_inc(chain, 1)
                dve.wait_ge(chain, 1)
                par(dve.tensor_copy(li[:], tn[:]))
                par(dve.tensor_scalar(f_hi[:], at(tn, SC), 192.0, 192.0, ALU.add, ALU.subtract))
                par(dve.tensor_tensor(f_lo[:], at(tn, SC), f_hi[:], ALU.subtract))
                dve.wait_ge(par_act, 4)
                par(dve.tensor_tensor(lr[:], lr[:], mag[:], ALU.mult))
                par(dve.tensor_tensor(li[:], li[:], mag[:], ALU.mult))
                par(dve.tensor_copy(rho[:], at(mag, SC)))
                par(dve.tensor_tensor(den[:], are[:], are[:], ALU.mult))
                par(dve.tensor_tensor(st[:], aim[:], aim[:], ALU.mult))
                par(dve.tensor_tensor(den[:], den[:], st[:], ALU.add))
                par(dve.reciprocal(den[:], den[:]))
                par(dve.tensor_scalar(nr[:], at(lr, 1), 1.0, None, ALU.subtract))
                par(dve.tensor_tensor(sr[:], nr[:], are[:], ALU.mult))
                par(dve.tensor_tensor(st[:], at(li, 1), aim[:], ALU.mult))
                par(dve.tensor_tensor(sr[:], sr[:], st[:], ALU.add))
                par(dve.tensor_tensor(sr[:], sr[:], den[:], ALU.mult))
                par(dve.tensor_tensor(si[:], at(li, 1), are[:], ALU.mult))
                par(dve.tensor_tensor(st[:], nr[:], aim[:], ALU.mult))
                par(dve.tensor_tensor(si[:], si[:], st[:], ALU.subtract))
                par(dve.tensor_tensor(si[:], si[:], den[:], ALU.mult))

            LINKS = 38

            def pair(p, r, first):
                n = [0]

                def link(ins):
                    n[0] += 1
                    ins.then_inc(chain, 1)
                    dve.wait_ge(chain, p * LINKS + (n[0] + 1))

                pc = ds(p, 1)
                power = lambda x, j0, nj: x[:, pc, j0:j0 + nj].rearrange("p a j -> p j a").to_broadcast([P, nj, GC])
                chan = lambda x, nj: x.to_broadcast([P, nj, GC])
                sin, cos = trig[:, 0], trig[:, 1]

                def matrices():
                    flat = lambda x: x[:, pc].rearrange("p a c -> p (a c)")
                    if not first:
                        dve.wait_ge(y_done, p)
                    link(dve.tensor_scalar(mt[:, 0], flat(bim), si[:, pc], None, ALU.mult))
                    link(dve.scalar_tensor_tensor(bb[:, 0], flat(bre), sr[:, pc], mt[:, 0], ALU.mult, ALU.subtract))
                    link(dve.tensor_scalar(mt[:, 0], flat(bim), sr[:, pc], None, ALU.mult))
                    link(dve.scalar_tensor_tensor(bb[:, 1], flat(bre), si[:, pc], mt[:, 0], ALU.mult, ALU.add))
                    rev = SC + 1
                    link(dve.tensor_tensor(X[:, 0], power(lr, rev, SC), chan(bb[:, 0:1], SC), ALU.mult))
                    link(dve.tensor_tensor(mt[:, 0:SC], power(li, rev, SC), chan(bb[:, 1:2], SC), ALU.mult))
                    link(dve.tensor_tensor(X[:, 0], X[:, 0], mt[:, 0:SC], ALU.subtract))
                    link(dve.tensor_tensor(X[:, 1], power(lr, rev, SC), chan(bb[:, 1:2], SC), ALU.mult))
                    link(dve.tensor_tensor(mt[:, 0:SC], power(li, rev, SC), chan(bb[:, 0:1], SC), ALU.mult))
                    link(dve.tensor_tensor(X[:, 1], X[:, 1], mt[:, 0:SC], ALU.add))
                    link(dve.tensor_tensor(Z[:, 0], power(lr, 0, SC + 1), chan(cre[:, pc], SC + 1), ALU.mult))
                    link(dve.tensor_tensor(mt[:], power(li, 0, SC + 1), chan(cim[:, pc], SC + 1), ALU.mult))
                    link(dve.tensor_tensor(Z[:, 0], Z[:, 0], mt[:], ALU.subtract))
                    link(dve.tensor_tensor(Z[:, 1], power(lr, 0, SC + 1), chan(cim[:, pc], SC + 1), ALU.mult))
                    link(dve.tensor_tensor(mt[:], power(li, 0, SC + 1), chan(cre[:, pc], SC + 1), ALU.mult))
                    link(dve.scalar_tensor_tensor(Z[:, 1].rearrange("p j c -> p (j c)"), Z[:, 1].rearrange("p j c -> p (j c)"),
                                                  -1.0, mt[:].rearrange("p j c -> p (j c)"), ALU.mult, ALU.subtract))
                    dve.sem_inc(xz_done, 1)

                def angles():
                    link(dve.tensor_scalar(t1[:], nn[:], f_hi[:, pc], None, ALU.mult))
                    link(dve.tensor_scalar(t2[:], t1[:], MAGIC, MAGIC, ALU.add, ALU.subtract))
                    link(dve.tensor_tensor(t1[:], t1[:], t2[:], ALU.subtract))
                    link(dve.scalar_tensor_tensor(t1[:], nn[:], f_lo[:, pc], t1[:], ALU.mult, ALU.add))
                    link(dve.tensor_scalar(t2[:], t1[:], MAGIC, MAGIC, ALU.add, ALU.subtract))
                    link(dve.tensor_tensor(sin, t1[:], t2[:], ALU.subtract))
                    link(dve.tensor_scalar(t1[:], sin, 0.25, None, ALU.add))
                    link(dve.tensor_scalar(t2[:], t1[:], MAGIC, MAGIC, ALU.add, ALU.subtract))
                    dve.tensor_tensor(cos, t1[:], t2[:], ALU.subtract).then_inc(ang_done, 1)

                def taps():
                    dve.wait_ge(mats_done, p + 1)
                    if not first:
                        dve.wait_ge(intra_in, p * 16 * SC)
                    for q in range(2):
                        src = py[q][0:GC, NCK:NCK + P]
                        dve.tensor_copy(msb[:, q, 1:SC].rearrange("c j d -> c (j d)"), src[:, GC:P])
                        dve.scalar_tensor_tensor(msb[:, q, 0], c["ident"][0:GC, 0:GC], dd[:, q, pc], src[:, 0:GC],
                                                 ALU.mult, ALU.add).then_inc(msb_done, 1)

                def states():
                    dve.wait_ge(trig_done, p + 1)
                    dve.wait_ge(pin_done, p + 1)
                    re, im = pin[:, 0:NCK], pin[:, NCK:2 * NCK]
                    link(dve.tensor_tensor(xt[:, 0], re, cos, ALU.mult))
                    link(dve.tensor_tensor(t1[:], im, sin, ALU.mult))
                    link(dve.tensor_tensor(xt[:, 0], xt[:, 0], t1[:], ALU.add))
                    link(dve.tensor_tensor(xt[:, 1], im, cos, ALU.mult))
                    link(dve.tensor_tensor(t2[:], re, sin, ALU.mult))
                    link(dve.tensor_tensor(xt[:, 1], xt[:, 1], t2[:], ALU.subtract))
                    for k in range(2):
                        link(dve.tensor_tensor_scan(xt[:, k], rho[:, pc].to_broadcast([P, NCK]), xt[:, k], 0.0, ALU.mult, ALU.add))
                    last = NCK - 1
                    link(dve.tensor_tensor(Hp[:, 0, 1:], xt[:, 0, 0:last], cos[:, 0:last], ALU.mult))
                    link(dve.tensor_tensor(t1[:, 0:last], xt[:, 1, 0:last], sin[:, 0:last], ALU.mult))
                    link(dve.tensor_tensor(Hp[:, 0, 1:], Hp[:, 0, 1:], t1[:, 0:last], ALU.subtract))
                    link(dve.tensor_tensor(Hp[:, 1, 1:], xt[:, 0, 0:last], sin[:, 0:last], ALU.mult))
                    link(dve.tensor_tensor(t2[:, 0:last], xt[:, 1, 0:last], cos[:, 0:last], ALU.mult))
                    link(dve.tensor_tensor(Hp[:, 1, 1:], Hp[:, 1, 1:], t2[:, 0:last], ALU.add))
                    assert n[0] == LINKS
                    dve.sem_inc(hp_done, 1)
                return matrices, angles, taps, states

            def body(b, p, r, first, last):
                if p is not None:
                    matrices, angles, taps, states = pair(p, r, first)
                    matrices()
                    angles()
                if p is None and b >= U_BLOCKS:
                    for t in range(NT):
                        e = b * NT + t
                        dve.wait_ge(sig_done, e - U_BLOCKS * NT + 1)
                        dve.tensor_tensor(stage[:, t], ps[t][:], stage[:, t], ALU.mult).then_inc(staged, 1)
                        if t == 0:
                            split_weights(b + 1, 1 - r)
                elif not last:
                    split_weights(b + 1, 1 - r)
                if p is not None:
                    taps()
                    states()

            split_weights(0, 0)
            parameters()
            dve.wait_ge(zeroed, 2)
            slots(dve, body)


def phase_dense(nc, c, tag, u_hi, u_lo, weights, kt, source, epilogue, out, in1=None, in2=None, sumsq=None,
                norm_g=None, rstd_of=None, permuted=False):
    nb = weights.shape[0]
    hk = kt // 2
    glu, gate, mul_add = epilogue == "glu", epilogue == "gate", epilogue == "mul_add"
    rows = nb // 2 if glu else nb
    with Bufs(nc, tag) as m:
        xa = m.sb("xa", [P, 2, hk, TT])
        raw = m.sb("raw", [P, 2, kt, P])
        w_hi = m.sb("w_hi", [P, 2, kt, P], F32R)
        w_lo = m.sb("w_lo", [P, 2, kt, P], F32R)
        ein = [m.sb(f"ein{k}", [P, 2, TT]) for k, x in enumerate((in1, in2)) if x is not None]
        res = m.sb("res", [P, 2, TT])
        sgb = m.sb("sgb", [P, NT, TT]) if glu else None
        sq = m.sb("sq", [P, TT]) if sumsq is not None else None
        rstd = m.sb("rstd", [P, NT, TT]) if norm_g is not None else None
        ps = [m.ps(f"ps{t}") for t in range(NT)]
        ms = [m.ps(f"ms{t}") for t in range(NT)] if norm_g is not None else None
        xa_in = [m.sem(f"xa_in{i}") for i in range(2)]
        raw_in = [m.sem(f"raw_in{i}") for i in range(2)]
        e_in = [[m.sem(f"e{k}_in{i}") for i in range(2)] for k in range(2)]
        ms_done, ln_done, rstd_done = m.sem("ms_d"), m.sem("ln_d"), m.sem("rstd_d")
        scaled, x_hi_done, x_lo_done = m.sem("scaled"), m.sem("x_hi"), m.sem("x_lo")
        w_hi_done, w_lo_done, proj_done = m.sem("w_hi_d"), m.sem("w_lo_d"), m.sem("proj")
        biased = m.sem("biased")
        gated = m.sem("gated")
        half = m.sem("half")
        done = m.sem("done")
        squared, summed = m.sem("squared"), m.sem("summed")
        stored = m.pool_dma_sem("stored")
        block = m.block()

        def blocks(engine, body):
            for q in range(2):
                body(q, 0, q, True, False)
            with engine.Fori(1, nb // 2 - 1) as i:
                for q in range(2):
                    body(i * 2 + q, i, q, False, False)
            for q in range(2):
                body(nb - 2 + q, nb // 2 - 1, q, False, True)

        @block.sync
        def _(sp):
            def load_weights(b, q):
                sp.dma_start(raw[:, q], weights[ds(b, 1)].rearrange("a p k c -> (a p) k c")).then_inc(raw_in[q], 16)

            def body(b, i, q, first, last):
                if not last:
                    sp.wait_ge(w_lo_done, b + 1)
                    load_weights(b + 2, q)
                row = i if glu else b
                for t in range(NT):
                    if not ein or (glu and q == 0):
                        continue
                    if not (first and (q == 0 or glu) and t < 2):
                        sp.wait_ge(done, row * NT + t - 1)
                    for k, x in enumerate((in1, in2)[:len(ein)]):
                        sp.dma_start(ein[k][:, t % 2], x(row, t)).then_inc(e_in[k][t % 2], 16)

            load_weights(0, 0)
            for n in range(2 * NT):
                if n >= 2:
                    sp.wait_ge(x_lo_done, n - 1)
                src = source(n % 2, n // 2)
                if permuted:
                    for k in range(hk):
                        sp.dma_start(xa[:, n % 2, k], src[k]).then_inc(xa_in[n % 2], 16)
                else:
                    sp.dma_start(xa[:, n % 2], src).then_inc(xa_in[n % 2], 16)
                if n == 1:
                    load_weights(1, 1)
            blocks(sp, body)

        @block.gpsimd
        def _(pool):
            def body(b, i, q, first, last):
                row = i if glu else b
                for t in range(NT):
                    if glu and q == 0:
                        continue
                    pool.wait_ge(done, row * NT + t + 1)
                    pool.dma_start(out[ds(row, 1), :, t * TT:(t + 1) * TT].rearrange("a p n -> (a p) n"),
                                   res[:, t % 2]).then_inc(stored, 16)
                    pool.wait_ge(stored, (row * NT + t) * 16 + 16)
            blocks(pool, body)

        @block.tensor
        def _(pe):
            def body(b, i, q, first, last):
                pe.wait_ge(w_lo_done, b + 1)
                for t in range(NT):
                    if first and q == 0:
                        pe.wait_ge(x_lo_done, 2 * t + 2)
                    elif glu and q == 1:
                        pe.wait_ge(biased, i * NT + t + 1)
                    elif glu:
                        pe.wait_ge(half, (i - 1) * NT + t + 1)
                    else:
                        pe.wait_ge(half if gate or mul_add else done, (b - 1) * NT + t + 1)
                    at = slice(t * TT, (t + 1) * TT)
                    for k in range(kt):
                        ins = split_matmuls(pe, ps[t][:], w_hi[:, q, k], w_lo[:, q, k], u_hi[:, k, at], u_lo[:, k, at],
                                            k == 0, k == kt - 1)
                    ins.then_inc(proj_done, 1)

            if norm_g is not None:
                for t in range(NT):
                    pe.matmul(ms[t][:], c["ones"][:], rstd_of[:, t], start=True, stop=True).then_inc(ms_done, 1)
            blocks(pe, body)

        def tiles(buf, n):
            x = buf[:, n % 2 * hk:(n % 2 + 1) * hk, n // 2 * TT:(n // 2 + 1) * TT]
            return x

        @block.scalar
        def _(act):
            def round_weights(b, i, q):
                act.wait_ge(raw_in[q], i * 16 + 16)
                act.activation(w_hi[:, q], raw[:, q], ACT.Copy).then_inc(w_hi_done, 1)

            def body(b, i, q, first, last):
                for t in range(NT):
                    e = b * NT + t
                    act.wait_ge(proj_done, e + 1)
                    if epilogue == "copy":
                        if not (first and q == 0 and t < 2):
                            act.wait_ge(stored, e * 16 - 16)
                        act.activation(res[:, t % 2], ps[t][:], ACT.Copy).then_inc(done, 1)
                    if glu and q == 0:
                        act.wait_ge(biased, i * NT + t + 1)
                        act.activation(sgb[:, t], sgb[:, t], ACT.Sigmoid).then_inc(gated, 1)
                    if gate:
                        if not (first and q == 0 and t < 2):
                            act.wait_ge(stored, e * 16 - 16)
                            if sumsq is not None:
                                act.wait_ge(squared, e - 1)
                        act.activation(res[:, t % 2], ps[t][:], ACT.Sigmoid).then_inc(half, 1)
                    if t == 0 and not (last and q == 1):
                        round_weights(b + 1, i + q, 1 - q)
                    if sumsq is not None:
                        act.wait_ge(done, e + 1)
                        if not (first and q == 0 and t == 0):
                            act.wait_ge(summed, e)
                        act.activation(sq[:], res[:, t % 2], ACT.Square).then_inc(squared, 1)

            round_weights(0, 0, 0)
            if norm_g is not None:
                act.preload_act_table_set("natural_log_exp_and_others")
                for t in range(NT):
                    act.wait_ge(ms_done, t + 1)
                    act.activation(rstd[:, t], ms[t][:], ACT.Ln, scale=1.0 / D, bias=c["eps"][:]).then_inc(ln_done, 1)
                    act.wait_ge(ln_done, t + 1)
                    act.activation(rstd[:, t], rstd[:, t], ACT.Exp, scale=-0.5).then_inc(rstd_done, 1)
            for n in range(2 * NT):
                if norm_g is None:
                    act.wait_ge(xa_in[n % 2], 16 * (n // 2 + 1) * (hk if permuted else 1))
                else:
                    act.wait_ge(scaled, n * hk + hk)
                for k in range(hk):
                    src, dst = xa[:, n % 2, k], tiles(u_hi, n)[:, k]
                    if permuted:
                        src = src.rearrange("p (j n) -> p n j", j=SC)
                        dst = dst.rearrange("p (n j) -> p n j", j=SC)
                    act.activation(dst, src, ACT.Copy).then_inc(x_hi_done, 1)
            blocks(act, body)

        @block.vector
        def _(dve):
            def split_weights(b, q):
                dve.wait_ge(w_hi_done, b + 1)
                dve.tensor_tensor(w_lo[:, q], raw[:, q], w_hi[:, q].bitcast(F32), ALU.subtract).then_inc(w_lo_done, 1)

            def add_square(e, t, start):
                dve.wait_ge(squared, e + 1)
                if start:
                    dve.tensor_copy(sumsq[:, t], sq[:]).then_inc(summed, 1)
                else:
                    dve.tensor_tensor(sumsq[:, t], sumsq[:, t], sq[:], ALU.add).then_inc(summed, 1)

            def body(b, i, q, first, last):
                for t in range(NT):
                    e = b * NT + t
                    row = i if glu else b
                    g = row * NT + t
                    early = first and (q == 0 or glu) and t < 2
                    r = res[:, t % 2]

                    def take(k):
                        dve.wait_ge(e_in[k][t % 2], (row * 2 + t // 2) * 16 + 16)

                    if glu and q == 0:
                        if not first:
                            dve.wait_ge(done, (i - 1) * NT + t + 1)
                        dve.wait_ge(proj_done, e + 1)
                        dve.tensor_scalar(sgb[:, t], ps[t][:], c["b_glu"][:, ds(i + nb // 2, 1)], None, ALU.add).then_inc(biased, 1)
                    elif glu:
                        if not early:
                            dve.wait_ge(stored, g * 16 - 16)
                        dve.wait_ge(gated, i * NT + t + 1)
                        dve.wait_ge(proj_done, e + 1)
                        dve.scalar_tensor_tensor(r, ps[t][:], c["b_glu"][:, ds(i, 1)], sgb[:, t], ALU.add, ALU.mult).then_inc(half, 1)
                        take(0)
                        dve.wait_ge(half, g + 1)
                        dve.tensor_tensor(r, r, ein[0][:, t % 2], ALU.mult).then_inc(done, 1)
                    elif gate:
                        take(0)
                        dve.wait_ge(half, g + 1)
                        dve.tensor_tensor(r, r, ein[0][:, t % 2], ALU.mult).then_inc(biased, 1)
                        take(1)
                        dve.wait_ge(biased, g + 1)
                        dve.tensor_tensor(r, r, ein[1][:, t % 2], ALU.add).then_inc(done, 1)
                    elif epilogue != "copy":
                        if not early:
                            dve.wait_ge(stored, g * 16 - 16)
                            if sumsq is not None:
                                dve.wait_ge(squared, g - 1)
                        take(0)
                        dve.wait_ge(proj_done, e + 1)
                        op = ALU.add if epilogue == "add" else ALU.mult
                        dve.tensor_tensor(r, ps[t][:], ein[0][:, t % 2], op).then_inc(half if mul_add else done, 1)
                        if mul_add:
                            take(1)
                            dve.wait_ge(half, g + 1)
                            dve.tensor_tensor(r, r, ein[1][:, t % 2], ALU.add).then_inc(done, 1)
                    if sumsq is not None:
                        add_square(e, t, first and q == 0)
                    if t == 0 and not (last and q == 1):
                        split_weights(b + 1, 1 - q)

            split_weights(0, 0)
            for n in range(2 * NT):
                t = n // 2
                if norm_g is not None:
                    dve.wait_ge(xa_in[n % 2], 16 * (n // 2 + 1))
                    dve.wait_ge(rstd_done, t + 1)
                    for k in range(hk):
                        g = n % 2 * hk + k
                        dve.scalar_tensor_tensor(xa[:, n % 2, k], xa[:, n % 2, k], norm_g[:, g:g + 1], rstd[:, t],
                                                 ALU.mult, ALU.mult).then_inc(scaled, 1)
                for k in range(hk):
                    dve.wait_ge(x_hi_done, n * hk + k + 1)
                    src, hi, lo = xa[:, n % 2, k], tiles(u_hi, n)[:, k].bitcast(F32), tiles(u_lo, n)[:, k]
                    if permuted:
                        src = src.rearrange("p (j n) -> p n j", j=SC)
                        hi, lo = (x.rearrange("p (n j) -> p n j", j=SC) for x in (hi, lo))
                    ins = dve.tensor_tensor(lo, src, hi, ALU.subtract)
                ins.then_inc(x_lo_done, 1)
            blocks(dve, body)


def phase_final(nc, c, a, sumsq, h2, out):
    with Bufs(nc, "fin") as m:
        hx = m.sb("hx", [P, 4, SEQ])
        rstd = m.sb("rstd", [P, NT, TT])
        ms = [m.ps(f"ms{t}") for t in range(NT)]
        h_in = [m.sem(f"h_in{i}") for i in range(4)]
        ms_done, ln_done, rstd_done, scaled = m.sem("ms_d"), m.sem("ln_d"), m.sem("rstd_d"), m.sem("scaled")
        stored = [m.sem(f"stored{i}") for i in range(4)]
        block = m.block()

        @block.sync
        def _(sp):
            for k in range(KT):
                if k >= 4:
                    sp.wait_ge(stored[k % 4], 16)
                sp.dma_start(hx[:, k % 4], h2[k]).then_inc(h_in[k % 4], 16)

        @block.tensor
        def _(pe):
            for t in range(NT):
                pe.matmul(ms[t][:], c["ones"][:], sumsq[:, t], start=True, stop=True).then_inc(ms_done, 1)

        @block.scalar
        def _(act):
            act.preload_act_table_set("natural_log_exp_and_others")
            for t in range(NT):
                act.wait_ge(ms_done, t + 1)
                act.activation(rstd[:, t], ms[t][:], ACT.Ln, scale=1.0 / D, bias=c["eps"][:]).then_inc(ln_done, 1)
                act.wait_ge(ln_done, t + 1)
                act.activation(rstd[:, t], rstd[:, t], ACT.Exp, scale=-0.5).then_inc(rstd_done, 1)
            for k in range(KT):
                act.wait_ge(scaled, k + 1)
                act.dma_start(out[k], hx[:, k % 4]).then_inc(stored[k % 4], 16)
            for i in range(4):
                act.wait_ge(stored[i], 16 * (KT // 4))

        @block.vector
        def _(dve):
            dve.wait_ge(rstd_done, NT)
            for k in range(KT):
                dve.wait_ge(h_in[k % 4], 16 * (k // 4 + 1))
                dve.scalar_tensor_tensor(hx[:, k % 4], hx[:, k % 4], c["fin_g"][:, k:k + 1],
                                         rstd[:].rearrange("p t n -> p (t n)"), ALU.mult, ALU.mult).then_inc(scaled, 1)


PHASES = ["norm_in", "hgrn", "s5", "glu"]


def build(nc, a):
    with ExitStack() as keep, Bufs(nc, "c") as m:
        Bufs.keep = keep
        c = dict(norm_g=m.sb("norm_g", [P, KT]), ple_g=m.sb("ple_g", [P, KT]), fin_g=m.sb("fin_g", [P, KT]),
                 hg_g=m.sb("hg_g", [P, HEADS]), b_glu=m.sb("b_glu", [P, KT]), lb=m.sb("lb", [P, HEADS]),
                 omlb=m.sb("omlb", [P, HEADS]), nomlb=m.sb("nomlb", [P, HEADS]), eps=m.sb("eps", [P, 1]),
                 ones=m.sb("ones", [P, P]), ident=m.sb("ident", [P, P]), causal=m.sb("causal", [P, P]),
                 restart=m.sb("restart", [P, TT]))
        with Bufs(nc, "u") as mu:
            u_hi = mu.sb("hi", [P, KT, SEQ], F32R)
            u_lo = mu.sb("lo", [P, KT, SEQ], F32R)
            if "norm_in" in PHASES:
                phase_norm_in(nc, c, a, u_hi, u_lo)
            if "hgrn" in PHASES:
                phase_hgrn(nc, c, a, u_hi, u_lo)
            if "s5" in PHASES:
                phase_s5(nc, c, a, u_hi, u_lo)

            def halves(x, kt):
                return lambda half, t: x[half * kt // 2:(half + 1) * kt // 2, :, t * TT:(t + 1) * TT].rearrange("k p n -> p k n")

            def tile_of(x):
                return lambda row, t: x[ds(row, 1), :, t * TT:(t + 1) * TT].rearrange("a p n -> (a p) n")

            def ys_halves(half, t):
                ys = a["ys"].rearrange("(k g) c j n -> k (g c) j n", k=S5KT)
                return ys[half * 2:half * 2 + 2, :, :, t * TT // SC:(t + 1) * TT // SC]

            x_tile = lambda row, t: a["x"][:, ds(row, 1), t * TT:(t + 1) * TT].rearrange("p a n -> p (a n)")
            if "glu" in PHASES:
                phase_dense(nc, c, "glu", u_hi, u_lo, a["w_glu"], S5KT, ys_halves, "glu", a["ys2"],
                            in1=tile_of(a["silu_z"]), permuted=True)
                phase_dense(nc, c, "os5", u_hi, u_lo, a["w_o_s5"], S5KT, halves(a["ys2"], S5KT), "mul", a["m_s5"],
                            in1=tile_of(a["gates"][KT:2 * KT]))
                phase_dense(nc, c, "ple", u_hi, u_lo, a["w_ple"], PLEKT, lambda half, t: a["p"][:, half:half + 1, t * TT:(t + 1) * TT],
                            "copy", a["pe"])
                phase_dense(nc, c, "ohg", u_hi, u_lo, a["w_o_hg"], KT, halves(a["o_gated"], KT), "mul_add", a["merged"],
                            in1=tile_of(a["gates"][0:KT]), in2=tile_of(a["m_s5"]))
                with Bufs(nc, "s") as msq:
                    sumsq = msq.sb("sumsq", [P, NT, TT])
                    phase_dense(nc, c, "out", u_hi, u_lo, a["w_out"], KT, halves(a["merged"], KT), "add", a["h"],
                                in1=x_tile, sumsq=sumsq)
                    phase_dense(nc, c, "pg", u_hi, u_lo, a["w_ple_gate"], KT, halves(a["h"], KT), "gate", a["h2"],
                                in1=tile_of(a["pe"]), in2=tile_of(a["h"]), sumsq=sumsq, norm_g=c["ple_g"], rstd_of=sumsq)
                    phase_final(nc, c, a, sumsq, a["h2"], a["out"])


SCRATCH = dict(o_gated=(HEADS, P, SEQ), us=(GRP, GC, SC, NCK), ys=(GRP, GC, SC, NCK), silu_z=(S5KT, P, SEQ),
               gates=(2 * KT, P, SEQ), ys2=(S5KT, P, SEQ), m_s5=(KT, P, SEQ), pe=(KT, P, SEQ), merged=(KT, P, SEQ),
               h=(KT, P, SEQ), h2=(KT, P, SEQ))


def columns(v):
    return v.reshape(-1, P).T


def weight_blocks(w):
    k, n = w.shape
    return w.reshape(k // P, P, n // P, P).transpose(2, 1, 0, 3)


def time_last(v):
    return v.T.reshape(-1, P, v.shape[0]).transpose(1, 0, 2)


def state_pairs(v):
    v = v.reshape((PAIRS, 2, NS) + v.shape[2:])
    return v.transpose((1, 2, 0) + tuple(range(3, v.ndim))).reshape((P, PAIRS) + v.shape[3:])


def kernel(x, p, norm_g, w_in, hg_lb, hg_norm_g, w_o_hg, s5_a_re, s5_a_im, s5_log_dt, s5_b_re, s5_b_im, s5_c_re, s5_c_im,
           s5_d, w_glu, b_glu, w_o_s5, w_out, ple_norm_g, w_ple, w_ple_gate, final_norm_g):
    import numpy as np
    import concourse.bacc as bacc
    from concourse.bass_utils import run_bass_kernel_spmd

    glu = weight_blocks(w_glu[0])
    half = glu.shape[0] // 2
    laid_out = dict(
        x=time_last(x[0]), p=time_last(p[0, 0]), norm_g=columns(norm_g[0]), w_in=weight_blocks(w_in[0]),
        hg_lb=hg_lb.reshape(2, HEADS, P).transpose(2, 0, 1), hg_norm_g=columns(hg_norm_g[0]), w_o_hg=weight_blocks(w_o_hg[0]),
        s5_a_re=state_pairs(s5_a_re[0]), s5_a_im=state_pairs(s5_a_im[0]), s5_log_dt=s5_log_dt[0].reshape(PAIRS, 2).T,
        s5_b_re=state_pairs(s5_b_re[0]), s5_b_im=state_pairs(s5_b_im[0]),
        s5_c_re=state_pairs(s5_c_re[0].transpose(0, 2, 1)), s5_c_im=state_pairs(s5_c_im[0].transpose(0, 2, 1)),
        s5_d=s5_d[0].reshape(PAIRS, 2, GC).transpose(2, 1, 0),
        w_glu=np.stack([glu[half:], glu[:half]], axis=1).reshape(glu.shape), b_glu=columns(b_glu[0]),
        w_o_s5=weight_blocks(w_o_s5[0]), w_out=weight_blocks(w_out[0]), ple_norm_g=columns(ple_norm_g[0]),
        w_ple=weight_blocks(w_ple[0]), w_ple_gate=weight_blocks(w_ple_gate[0]), final_norm_g=columns(final_norm_g))
    nc = bacc.Bacc("TRN2", target_bir_lowering=False, num_devices=1)
    arrays, dram = {}, {}
    for name, v in laid_out.items():
        arrays[f"{name}_in"] = np.ascontiguousarray(v)
        dram[name] = nc.dram_tensor(f"{name}_in", v.shape, F32, kind="ExternalInput").ap()
    for name, shape in SCRATCH.items():
        dram[name] = nc.dram_tensor(f"{name}_scratch", shape, F32, kind="Internal").ap()
    dram["out"] = nc.dram_tensor("out_t", (KT, P, SEQ), F32, kind="ExternalOutput").ap()
    build(nc, dram)
    result = run_bass_kernel_spmd(nc, [arrays], core_ids=[0]).results[0]["out_t"]
    return np.ascontiguousarray(result.reshape(D, SEQ).T).reshape(x.shape)
```

```python
from contextlib import ExitStack

import concourse.bass as bass
from concourse import mybir

F32 = mybir.dt.float32
F32R = mybir.dt.float32r
U32 = mybir.dt.uint32
ALU = mybir.AluOpType
ACT = mybir.ActivationFunctionType
ds = bass.ds

P = 128
SEQ = 2048
D = 1024
KT = D // P
TT = 512
NT = SEQ // TT
HEADS = 8
CH = 64
NCH = TT // CH
NPAIR = TT // P
EPS = 1e-6
S5W = 512
S5KT = S5W // P
PLE = 256
PLEKT = PLE // P
GRP = 32
GC = 16
NS = 64
SC = 8
NCK = SEQ // SC
PAIRS = GRP // 2
TWO_PI = 6.283185
MAGIC = 12582912.0
QB, FB, IB, GB = 0, 8, 16, 24
UB, ZB, HB, SB = 32, 36, 40, 48


class Bufs:

    keep = None

    def __init__(self, nc, tag):
        self.nc, self.tag, self.stack, self.nums = nc, tag, ExitStack(), []

    def __enter__(self):
        self.stack.__enter__()
        return self

    def __exit__(self, *a):
        return self.stack.__exit__(*a)

    def sb(self, name, shape, dt=F32):
        return self.stack.enter_context(self.nc.sbuf_tensor(f"{self.tag}_{name}", shape, dt))

    def ps(self, name, shape=(P, TT)):
        return self.stack.enter_context(self.nc.psum_tensor(f"{self.tag}_{name}", list(shape), F32))

    def sem(self, name):
        s = self.stack.enter_context(self.nc.semaphore(f"{self.tag}_{name}"))
        self.nums.append(s.num)
        return s

    def pool_dma_sem(self, name):
        return self.keep.enter_context(self.nc.semaphore(f"{self.tag}_{name}"))

    def clear(self):
        nums = sorted(self.nums)
        starts = [n for n in nums if n - 1 not in nums]
        ends = [n for n in nums if n + 1 not in nums]
        for lo, hi in zip(starts, ends):
            self.nc.gpsimd.sem_clear(range(lo, hi + 1))
        self.nc.all_engine_barrier()

    def block(self):
        self.stack.callback(self.clear)
        return self.stack.enter_context(self.nc.Block())


def split_matmuls(pe, out, w_hi, w_lo, u_hi, u_lo, first, last):
    pe.matmul(out, w_hi, u_hi, start=first, stop=False)
    pe.matmul(out, w_hi, u_lo, start=False, stop=False)
    return pe.matmul(out, w_lo, u_hi, start=False, stop=last)


def prefetch(sp, c, blocks):
    for half, src in enumerate(blocks):
        dst = c["raw"][:, half]
        if len(src.shape) == 4:
            dst, src = dst.rearrange("p (b k) c -> p b k c", b=src.shape[0]), src.rearrange("b p k c -> p b k c")
        sp.dma_start(dst, src).then_inc(c["prefetched"][half], 16)


def prefetched(sp, c, number, raw_in):
    for half in range(2):
        sp.wait_ge(c["prefetched"][half], 16 * number + 16)
        sp.sem_inc(raw_in[half], 16)


def phase_norm_in(nc, c, a, u_hi, u_lo):
    FIRST = 4
    with Bufs(nc, "n0") as m:
        xs = m.sb("xs", [P, 3, KT, TT])
        sq = m.sb("sq", [P, 2, TT])
        rstd = m.sb("rstd", [P, 2, TT])
        u = m.sb("u", [P, 4, TT])
        lb2 = m.sb("lb2", [P, 2, HEADS])
        lbm = m.sb("lbm", [P, HEADS])
        lbs = m.sb("lbs", [P, HEADS])
        ms = m.ps("ms", (P, NT, TT))
        first_in, x_in = [m.sem(f"first_in{i}") for i in range(FIRST)], [m.sem(f"x_in{i}") for i in range(1, NT)]
        small_in = m.sem("small_in")
        sq_done, ms_done, ln_done, rstd_done = (m.sem(n) for n in ("sq", "ms", "ln", "rstd"))
        u_done, hi_done, lo_done = (m.sem(n) for n in ("u", "hi", "lo"))
        ones_done, lb_done, lbe_done = m.sem("ones"), m.sem("lb"), m.sem("lbe")
        mk = m.sem("masks")
        block = m.block()

        @block.sync
        def _(sp):
            for i in range(FIRST):
                ks = slice(i * KT // FIRST, (i + 1) * KT // FIRST)
                sp.dma_start(xs[:, 0, ks], a["x"][:, ks, 0:TT]).then_inc(first_in[i], 16)
            for dst, src in ((c["norm_g"][:], a["norm_g"]), (c["ple_g"][:], a["ple_norm_g"]),
                             (c["fin_g"][:], a["final_norm_g"]), (c["hg_g"][:], a["hg_norm_g"]),
                             (c["b_glu"][:], a["b_glu"]), (lb2[:], a["hg_lb"])):
                sp.dma_start(dst, src).then_inc(small_in, 16)
            for t in range(1, NT):
                if t >= 3:
                    sp.wait_ge(u_done, KT * (t - 2))
                sp.dma_start(xs[:, t % 3], a["x"][:, :, t * TT:(t + 1) * TT]).then_inc(x_in[t - 1], 16)
            prefetch(sp, c, [a["w_in"][FB], a["w_in"][GB]])

        @block.gpsimd
        def _(pool):
            pool.memset(c["ones"][:], 1.0).then_inc(ones_done, 1)
            pool.memset(c["ident"][:], 0.0).then_inc(mk, 1)
            pool.memset(c["causal"][:], 1.0).then_inc(mk, 1)
            pool.memset(c["restart"][:], 1.0).then_inc(mk, 1)
            pool.wait_ge(mk, 3)
            pool.affine_select(out=c["ident"][:], in_=c["ident"][:], compare_op=ALU.not_equal, fill=1.0,
                               base=0, pattern=[[-1, P]], channel_multiplier=1).then_inc(mk, 1)
            pool.affine_select(out=c["causal"][:], in_=c["causal"][:], compare_op=ALU.is_ge, fill=0.0,
                               base=0, pattern=[[1, P]], channel_multiplier=-1).then_inc(mk, 1)
            pool.memset(c["restart"][:].rearrange("p (n j) -> p n j", j=CH)[:, :, 0:1], 0.0).then_inc(mk, 1)
            pool.wait_ge(mk, 5)
            pool.memset(c["causal"][0:CH, CH:P], 0.0).then_inc(mk, 1)

        @block.tensor
        def _(pe):
            pe.wait_ge(ones_done, 1)
            for n in range(NT * KT):
                t, k = n // KT, n % KT
                pe.wait_ge(sq_done, n + 1)
                pe.matmul(ms[:, t], c["ones"][:], sq[:, n % 2], start=k == 0, stop=k == KT - 1).then_inc(ms_done, 1)

        @block.scalar
        def _(act):
            def square(n):
                t, k = n // KT, n % KT
                if t == 0 and k % (KT // FIRST) == 0:
                    act.wait_ge(first_in[k // (KT // FIRST)], 16)
                elif k == 0:
                    act.wait_ge(x_in[t - 1], 16)
                if n >= 2:
                    act.wait_ge(ms_done, n - 1)
                act.activation(sq[:, n % 2], xs[:, t % 3, k], ACT.Square).then_inc(sq_done, 1)

            def one_over_rms(t):
                act.wait_ge(ms_done, KT * (t + 1))
                if t >= 2:
                    act.wait_ge(u_done, KT * (t - 1))
                act.activation(rstd[:, t % 2], ms[:, t], ACT.Ln, scale=1.0 / D, bias=c["eps"][:]).then_inc(ln_done, 1)
                act.wait_ge(ln_done, t + 1)
                act.activation(rstd[:, t % 2], rstd[:, t % 2], ACT.Exp, scale=-0.5).then_inc(rstd_done, 1)

            for k in range(KT):
                square(k)
            act.preload_act_table_set("natural_log_exp_and_others")
            act.wait_ge(lb_done, 1)
            one_over_rms(0)
            act.wait_ge(lb_done, 3)
            act.activation(lb2[:], lb2[:], ACT.Exp).then_inc(lbe_done, 1)
            for t in range(NT):
                for k in range(KT):
                    n = t * KT + k
                    act.wait_ge(u_done, n + 1)
                    act.activation(u_hi[:, k, t * TT:(t + 1) * TT], u[:, n % 4], ACT.Copy).then_inc(hi_done, 1)
                    if t + 1 < NT and k < KT // 2:
                        square(t * KT + KT + 2 * k)
                        square(t * KT + KT + 2 * k + 1)
                    if t + 1 < NT and k == KT - 2:
                        one_over_rms(t + 1)

        @block.vector
        def _(dve):
            def split_lo(n):
                t, k = n // KT, n % KT
                dve.wait_ge(hi_done, n + 1)
                at = slice(t * TT, (t + 1) * TT)
                dve.tensor_tensor(u_lo[:, k, at], u[:, n % 4], u_hi[:, k, at].bitcast(F32), ALU.subtract).then_inc(lo_done, 1)

            dve.memset(c["eps"][:], EPS).then_inc(lb_done, 1)
            dve.wait_ge(small_in, 16 * 6)
            dve.tensor_tensor(lbm[:], lb2[:, 0], lb2[:, 1], ALU.max).then_inc(lb_done, 1)
            dve.wait_ge(lb_done, 2)
            dve.tensor_tensor(lb2[:], lb2[:], lbm[:].rearrange("p (a h) -> p a h", a=1).to_broadcast([P, 2, HEADS]),
                              ALU.subtract).then_inc(lb_done, 1)
            for t in range(NT):
                dve.wait_ge(rstd_done, t + 1)
                for k in range(KT):
                    n = t * KT + k
                    if n >= 4:
                        dve.wait_ge(lo_done, n - 3)
                    dve.scalar_tensor_tensor(u[:, n % 4], xs[:, t % 3, k], c["norm_g"][:, k:k + 1], rstd[:, t % 2],
                                             ALU.mult, ALU.mult).then_inc(u_done, 1)
                    if n >= 2:
                        split_lo(n - 2)
                if t == 0:
                    dve.wait_ge(lbe_done, 1)
                    dve.tensor_tensor(lbs[:], lb2[:, 0], lb2[:, 1], ALU.add).then_inc(lb_done, 1)
                    dve.wait_ge(lb_done, 4)
                    dve.reciprocal(lbs[:], lbs[:]).then_inc(lb_done, 1)
                    dve.wait_ge(lb_done, 5)
                    dve.tensor_tensor(c["lb"][:], lb2[:, 0], lbs[:], ALU.mult).then_inc(lb_done, 1)
                    dve.wait_ge(lb_done, 6)
                    dve.tensor_scalar(c["omlb"][:], c["lb"][:], -1.0, 1.0, ALU.mult, ALU.add).then_inc(lb_done, 1)
                    dve.tensor_scalar(c["nomlb"][:], c["lb"][:], 1.0, None, ALU.subtract).then_inc(lb_done, 1)
            split_lo(NT * KT - 2)
            split_lo(NT * KT - 1)


def phase_hgrn(nc, c, a, u_hi, u_lo):
    STEPS = HEADS * NT
    KIND = [FB, GB, IB, QB]
    with Bufs(nc, "hg") as m:
        raw = c["raw"]
        w_hi = m.sb("w_hi", [P, 4, KT, P], F32R)
        w_lo = m.sb("w_lo", [P, 4, KT, P], F32R)
        sig = m.sb("sig", [P, TT])
        lf = m.sb("lf", [P, TT])
        b = m.sb("b", [P, TT])
        qe = m.sb("qe", [P, TT])
        ke = m.sb("ke", [P, TT])
        iv = m.sb("iv", [P, TT])
        sg = m.sb("sg", [P, 2, TT])
        ken = m.sb("ken", [P, NPAIR, P])
        ivn = m.sb("ivn", [P, NPAIR, P])
        sT = m.sb("sT", [P, NPAIR, P])
        osq = m.sb("osq", [P, TT])
        osq_hi, osq_lo = m.sb("osq_hi", [P, TT], F32R), m.sb("osq_lo", [P, TT], F32R)
        ones_r = m.sb("ones_r", [P, P], F32R)
        y = m.sb("y", [P, TT])
        S = m.sb("S", [P, NCH, P])
        G = m.sb("G", [P, P])
        R = m.sb("R", [P, NCH + 1])
        coef = m.sb("coef", [P, NCH])
        pf, pg, pi, pq = (m.ps(n) for n in ("pf", "pg", "pi", "pq"))
        pk, pv, psc, po = (m.ps(n) for n in ("pk", "pv", "psc", "po"))
        raw_in = [m.sem(f"raw_in{i}") for i in range(2)]
        w_hi_done, w_lo_done, proj_done = m.sem("w_hi"), m.sem("w_lo"), m.sem("proj")
        turned, kv_done, o_done, ms_done = (m.sem(n) for n in ("turned", "kv", "o", "ms"))
        sigf, sigg, iv_done, lf_done = (m.sem(n) for n in ("sigf", "sigg", "ivc", "lfd"))
        coef_done, e2_done, e1_done = m.sem("coefd"), m.sem("e2"), m.sem("e1")
        ivn_done, osq_done, ln_done, rstd_done = (m.sem(n) for n in ("ivn", "osqd", "ln", "rstdd"))
        ken_done, masked, states, sg_done = (m.sem(n) for n in ("kend", "masked", "states", "sgd"))
        lfin_done, scan_done, arg_done, d_done = (m.sem(n) for n in ("lfin", "scan", "arg", "d"))
        ke_done, qe_done, yn_done, y_done = (m.sem(n) for n in ("ked", "qed", "yn", "yd"))
        r_done, g_done = m.sem("r"), m.sem("g")
        osq_hi_done, osq_lo_done, ones_done = m.sem("osq_hi_d"), m.sem("osq_lo_d"), m.sem("ones_d")
        zeroed, o_out, last_out = m.sem("zeroed"), m.pool_dma_sem("o_out"), m.sem("last_out")
        block = m.block()

        def heads(engine, head):
            head(0, True, False)
            with engine.Fori(1, HEADS - 1) as h:
                head(h, False, False)
            head(HEADS - 1, False, True)

        @block.sync
        def _(sp):
            def head(h, first, last):
                for kind in range(2 if first else 0, 4):
                    sp.wait_ge(w_lo_done, h * 4 + kind - 1)
                    sp.dma_start(raw[:, kind % 2], a["w_in"][ds(h + KIND[kind], 1)].rearrange("a p k c -> (a p) k c")
                                 ).then_inc(raw_in[kind % 2], 16)
            prefetched(sp, c, 0, raw_in)
            heads(sp, head)
            sp.wait_ge(w_lo_done, HEADS * 4)
            prefetch(sp, c, [a["w_in"][UB], a["w_in"][UB + 1]])
            sp.wait_ge(y_done, STEPS)
            sp.dma_start(a["o_gated"][HEADS - 1, :, (NT - 1) * TT:], y[:]).then_inc(last_out, 16)
            sp.wait_ge(last_out, 16)

        @block.gpsimd
        def _(pool):
            def head(h, first, last):
                for t in range(NT - 1 if last else NT):
                    pool.wait_ge(y_done, h * NT + t + 1)
                    pool.dma_start(a["o_gated"][ds(h, 1), :, t * TT:(t + 1) * TT].rearrange("a p n -> (a p) n"),
                                   y[:]).then_inc(o_out, 16)
            pool.memset(sT[:], 0.0).then_inc(zeroed, 1)
            heads(pool, head)
            pool.wait_ge(o_out, 16 * STEPS - 16)

        @block.tensor
        def _(pe):
            def project(n, t, kind, new_weights):
                if new_weights:
                    pe.wait_ge(w_lo_done, n + kind + 1)
                out = (pf, pg, pi, pq)[kind]
                at = slice(t * TT, (t + 1) * TT)
                for k in range(KT):
                    ins = split_matmuls(pe, out[:], w_hi[:, kind, k], w_lo[:, kind, k], u_hi[:, k, at], u_lo[:, k, at],
                                        k == 0, k == KT - 1)
                ins.then_inc(proj_done, 1)

            def turn(s, first):
                pe.wait_ge(ke_done, s + 1)
                if not first:
                    pe.wait_ge(g_done, s * NCH)
                for p in range(NPAIR):
                    at = slice(p * P, (p + 1) * P)
                    pe.transpose(pk[:, at], ke[:, at], c["ident"][:]).then_inc(turned, 1)
                pe.wait_ge(iv_done, s + 1)
                for p in range(NPAIR):
                    at = slice(p * P, (p + 1) * P)
                    pe.transpose(pv[:, at], iv[:, at], c["ident"][:]).then_inc(turned, 1)
                pe.wait_ge(qe_done, s + 1)
                if not first:
                    pe.wait_ge(ln_done, s)
                for p in range(NPAIR):
                    at = slice(p * P, (p + 1) * P)
                    pe.matmul(psc[:, at], ke[:, at], qe[:, at], start=True, stop=True).then_inc(turned, 1)

            def outer(s):
                pe.wait_ge(ken_done, s + 1)
                pe.wait_ge(ivn_done, s + 1)
                for j in range(NCH):
                    rows = slice(j % 2 * CH, j % 2 * CH + CH)
                    out = (pk, pv)[j % 2][:, j // 2 * P:j // 2 * P + P]
                    ins = pe.matmul(out, ken[rows, j // 2], ivn[rows, j // 2], start=True, stop=True)
                ins.then_inc(kv_done, 1)

            def attend(s, first):
                pe.wait_ge(masked, s + 1)
                if not first:
                    pe.wait_ge(yn_done, s)
                for p in range(NPAIR):
                    for j in (2 * p, 2 * p + 1):
                        pe.wait_ge(states, s * NCH + j + 1)
                        at = slice(j * CH, (j + 1) * CH)
                        pe.matmul(po[:, at], S[:, j], qe[:, at], start=j % 2 == 0, stop=False, skip_group_check=True)
                    pe.matmul(po[:, p * P:(p + 1) * P], ivn[:, p], sT[:, p], start=False, stop=True,
                              skip_group_check=True).then_inc(o_done, 1)

            def mean_square(s):
                pe.wait_ge(osq_lo_done, s + 1)
                pe.matmul(psc[:], ones_r[:], osq_hi[:], start=True, stop=False)
                pe.matmul(psc[:], ones_r[:], osq_lo[:], start=False, stop=True).then_inc(ms_done, 1)

            def head(h, first, last):
                for t in range(NT):
                    n = h * NT + t
                    recur = not (first and t == 0)
                    if recur:
                        pe.wait_ge(sigf, n)
                    project(n, t, 0, t == 0)
                    if recur:
                        turn(n - 1, first and t == 1)
                        pe.wait_ge(sg_done, n)
                    project(n, t, 1, t == 0)
                    if recur:
                        outer(n - 1)
                    project(n, t, 2, t == 0)
                    if recur:
                        attend(n - 1, first and t == 1)
                    project(n, t, 3, t == 0)
                    if recur:
                        mean_square(n - 1)
            heads(pe, head)
            turn(STEPS - 1, False)
            outer(STEPS - 1)
            attend(STEPS - 1, False)
            mean_square(STEPS - 1)

        @block.scalar
        def _(act):
            def round_weights(h, kind):
                act.wait_ge(raw_in[kind % 2], (h * 2 + kind // 2 + 1) * 16)
                act.activation(w_hi[:, kind], raw[:, kind % 2], ACT.Copy).then_inc(w_hi_done, 1)

            def turned_iv(s):
                act.wait_ge(turned, s * 3 * NPAIR + 2 * NPAIR)
                act.activation(ivn[:].rearrange("p a n -> p (a n)"), pv[:], ACT.Copy).then_inc(ivn_done, 1)

            def norm(s, first):
                act.wait_ge(o_done, (s + 1) * NPAIR)
                if not first:
                    act.wait_ge(yn_done, s)
                act.activation(osq[:], po[:], ACT.Square).then_inc(osq_done, 1)
                act.wait_ge(osq_done, s + 1)
                act.activation(osq_hi[:], osq[:], ACT.Copy).then_inc(osq_hi_done, 1)
                act.wait_ge(ms_done, s + 1)
                act.activation(osq[:], psc[:], ACT.Ln, scale=1.0 / P, bias=c["eps"][:]).then_inc(ln_done, 1)
                act.wait_ge(ln_done, s + 1)
                act.activation(osq[:], osq[:], ACT.Exp, scale=-0.5).then_inc(rstd_done, 1)

            def head(h, first, last):
                for t in range(NT):
                    n = h * NT + t
                    recur = not (first and t == 0)
                    split = t == NT - 1 and not last
                    act.wait_ge(proj_done, n * 4 + 1)
                    if recur:
                        act.wait_ge(ke_done, n)
                    act.activation(sig[:], pf[:], ACT.Sigmoid).then_inc(sigf, 1)
                    if split:
                        round_weights(h + 1, 0)
                    if recur:
                        turned_iv(n - 1)
                    act.wait_ge(proj_done, n * 4 + 2)
                    if not first or t >= 2:
                        act.wait_ge(y_done, n - 1)
                    act.activation(sg[:, t % 2], pg[:], ACT.Sigmoid).then_inc(sigg, 1)
                    act.preload_act_table_set("natural_log_exp_and_others")
                    act.wait_ge(lfin_done, n + 1)
                    act.activation(lf[:], lf[:], ACT.Ln).then_inc(lf_done, 1)
                    if split:
                        round_weights(h + 1, 1)
                    act.wait_ge(arg_done, n + 1)
                    act.activation(coef[:], coef[:], ACT.Exp).then_inc(coef_done, 1)
                    act.wait_ge(d_done, n + 1)
                    act.activation(b[:], lf[:], ACT.Exp, scale=-1.0).then_inc(e2_done, 1)
                    act.activation(lf[:], lf[:], ACT.Exp).then_inc(e1_done, 1)
                    act.wait_ge(proj_done, n * 4 + 3)
                    act.activation(iv[:], pi[:], ACT.Copy).then_inc(iv_done, 1)
                    if split:
                        round_weights(h + 1, 2)
                    if recur:
                        norm(n - 1, first and t == 1)
                    if split:
                        act.wait_ge(proj_done, n * 4 + 4)
                        round_weights(h + 1, 3)

            act.activation(ones_r[:], c["ones"][:], ACT.Copy).then_inc(ones_done, 1)
            for kind in range(4):
                round_weights(0, kind)
            heads(act, head)
            turned_iv(STEPS - 1)
            norm(STEPS - 1, False)

        @block.vector
        def _(dve):
            mids = b[:].rearrange("p (n j) -> p n j", j=CH)[:, :, CH // 2 - 1:CH // 2]
            ends = b[:].rearrange("p (n j) -> p n j", j=CH)[:, :, CH - 1:CH]
            chunks = lambda x: x[:].rearrange("p (n j) -> p n j", j=CH)
            col = lambda x: x.rearrange("p (n a) -> p n a", a=1)

            def split_weights(h, kind):
                dve.wait_ge(w_hi_done, h * 4 + kind + 1)
                dve.tensor_tensor(w_lo[:, kind], raw[:, kind % 2], w_hi[:, kind].bitcast(F32),
                                  ALU.subtract).then_inc(w_lo_done, 1)

            def turned_scores(s):
                dve.wait_ge(turned, (s + 1) * 3 * NPAIR)
                dve.tensor_copy(ken[:].rearrange("p a n -> p (a n)"), pk[:]).then_inc(ken_done, 1)
                dve.copy_predicated(sT[:], c["causal"][:].rearrange("p (a n) -> p a n", a=1).to_broadcast([P, NPAIR, P]).bitcast(U32),
                                    psc[:].rearrange("p (a n) -> p a n", a=NPAIR)).then_inc(masked, 1)

            def carry_state(s, new_head):
                dve.wait_ge(kv_done, s + 1)
                for j in range(NCH):
                    kv = (pk, pv)[j % 2][:, j // 2 * P:j // 2 * P + P]
                    if new_head and j == 0:
                        dve.memset(S[:, 0], 0.0).then_inc(states, 1)
                        dve.wait_ge(states, s * NCH + 1)
                        dve.tensor_copy(G[:], kv).then_inc(g_done, 1)
                        continue
                    if j == 0:
                        dve.wait_ge(coef_done, s + 1)
                    dve.wait_ge(g_done, s * NCH + j)
                    dve.tensor_scalar(S[:, j], G[:], coef[:, j:j + 1], None, ALU.mult).then_inc(states, 1)
                    dve.wait_ge(states, s * NCH + j + 1)
                    dve.tensor_tensor(G[:], kv, S[:, j], ALU.add).then_inc(g_done, 1)

            def split_square(s):
                dve.wait_ge(osq_hi_done, s + 1)
                dve.tensor_tensor(osq_lo[:], osq[:], osq_hi[:].bitcast(F32), ALU.subtract).then_inc(osq_lo_done, 1)

            def gate(s, h, t):
                dve.wait_ge(rstd_done, s + 1)
                if not (isinstance(s, int) and s == 0):
                    dve.wait_ge(o_out, s * 16)
                dve.scalar_tensor_tensor(y[:], po[:], c["hg_g"][:, ds(h, 1)], osq[:], ALU.mult, ALU.mult).then_inc(yn_done, 1)
                dve.wait_ge(yn_done, s + 1)
                dve.tensor_tensor(y[:], y[:], sg[:, t % 2], ALU.mult).then_inc(y_done, 1)

            def head(h, first, last):
                for t in range(NT):
                    n = h * NT + t
                    recur = not (first and t == 0)
                    split = t == NT - 1 and not last
                    if recur:
                        dve.wait_ge(qe_done, n)
                    dve.wait_ge(sigf, n + 1)
                    dve.tensor_scalar(lf[:], sig[:], c["omlb"][:, ds(h, 1)], c["lb"][:, ds(h, 1)], ALU.mult,
                                      ALU.add).then_inc(lfin_done, 1)
                    if split:
                        split_weights(h + 1, 0)
                    if recur:
                        turned_scores(n - 1)
                        carry_state(n - 1, t == 1)
                    dve.wait_ge(sigg, n + 1)
                    dve.tensor_tensor(sg[:, t % 2], pg[:], sg[:, t % 2], ALU.mult).then_inc(sg_done, 1)
                    dve.wait_ge(lf_done, n + 1)
                    dve.tensor_tensor_scan(b[:], c["restart"][:], lf[:], 0.0, ALU.mult, ALU.add).then_inc(scan_done, 1)
                    if split:
                        split_weights(h + 1, 1)
                    dve.wait_ge(scan_done, n + 1)
                    dve.wait_ge(r_done, 2 * n + 1)
                    dve.tensor_tensor(col(R[:, 1:NCH + 1]), ends, mids, ALU.subtract).then_inc(r_done, 1)
                    dve.wait_ge(r_done, 2 * n + 2)
                    dve.tensor_tensor(col(coef[:]), col(R[:, 0:NCH]), mids, ALU.add).then_inc(arg_done, 1)
                    dve.tensor_tensor(chunks(lf), chunks(b), mids.to_broadcast([P, NCH, CH]), ALU.subtract).then_inc(d_done, 1)
                    dve.wait_ge(arg_done, n + 1)
                    dve.tensor_copy(R[:, 0:1], R[:, NCH:NCH + 1]).then_inc(r_done, 1)
                    dve.wait_ge(e2_done, n + 1)
                    dve.scalar_tensor_tensor(ke[:], sig[:], 1.0, b[:], ALU.subtract, ALU.mult).then_inc(ke_done, 1)
                    if split:
                        split_weights(h + 1, 2)
                    if recur:
                        split_square(n - 1)
                    dve.wait_ge(proj_done, n * 4 + 4)
                    dve.wait_ge(e1_done, n + 1)
                    dve.scalar_tensor_tensor(qe[:], pq[:], c["nomlb"][:, ds(h, 1)], lf[:], ALU.mult, ALU.mult).then_inc(qe_done, 1)
                    if recur:
                        gate(n - 1, h - 1 if t == 0 else h, (t - 1) % NT)
                    if split:
                        split_weights(h + 1, 3)

            for kind in range(4):
                split_weights(0, kind)
            dve.memset(R[:], 0.0).then_inc(r_done, 1)
            dve.wait_ge(zeroed, 1)
            heads(dve, head)
            turned_scores(STEPS - 1)
            carry_state(STEPS - 1, False)
            split_square(STEPS - 1)
            gate(STEPS - 1, HEADS - 1, NT - 1)


def phase_s5(nc, c, a, u_hi, u_lo):
    NB, U_BLOCKS, Z_BLOCKS = 24, S5KT, 2 * S5KT
    NL = 2 * SC + 1
    NW = NCK // NT
    with Bufs(nc, "s5") as m:
        raw = c["raw"]
        w_hi = m.sb("w_hi", [P, 2, KT, P], F32R)
        w_lo = m.sb("w_lo", [P, 2, KT, P], F32R)
        stage = m.sb("stage", [P, NT, TT])
        are, aim, dt = m.sb("are", [P, PAIRS]), m.sb("aim", [P, PAIRS]), m.sb("dt", [P, PAIRS])
        bre, bim = m.sb("bre", [P, PAIRS, GC]), m.sb("bim", [P, PAIRS, GC])
        cre, cim = m.sb("cre", [P, PAIRS, GC]), m.sb("cim", [P, PAIRS, GC])
        dd = m.sb("dd", [GC, 2, PAIRS])
        kk = m.sb("kk", [P, NL])
        nn = m.sb("nn", [P, NCK])
        adt, turns = m.sb("adt", [P, PAIRS]), m.sb("turns", [P, PAIRS])
        mag, tn = m.sb("mag", [P, PAIRS, NL]), m.sb("tn", [P, PAIRS, NL])
        lr, li = m.sb("lr", [P, PAIRS, NL]), m.sb("li", [P, PAIRS, NL])
        den, nr = m.sb("den", [P, PAIRS]), m.sb("nr", [P, PAIRS])
        sr, si, st = m.sb("sr", [P, PAIRS]), m.sb("si", [P, PAIRS]), m.sb("st", [P, PAIRS])
        rho = m.sb("rho", [P, PAIRS])
        f_hi, f_lo = m.sb("f_hi", [P, PAIRS]), m.sb("f_lo", [P, PAIRS])
        bb = m.sb("bb", [P, 2, GC])
        X = m.sb("X", [P, 2, SC, GC])
        Z = m.sb("Z", [P, 2, SC + 1, GC])
        mt = m.sb("mt", [P, SC + 1, GC])
        w_in_t = m.sb("w_in_t", [P, 2, P])
        msb = m.sb("msb", [GC, 2, SC, GC])
        w_intra = m.sb("w_intra", [P, 2, 2, P])
        U = m.sb("U", [P, 2, 2, NCK])
        trig = m.sb("trig", [P, 2, NCK])
        t1, t2 = m.sb("t1", [P, NCK]), m.sb("t2", [P, NCK])
        xt = m.sb("xt", [P, 2, NCK])
        Hp = m.sb("Hp", [P, 2, NCK])
        ysb = m.sb("ysb", [P, 2, 2, NCK])
        ps = [m.ps(f"ps{t}") for t in range(NT)]
        py = [m.ps(f"py{q}") for q in range(2)]
        px, pin = m.ps("px"), m.ps("pin")
        raw_in = [m.sem(f"raw_in{i}") for i in range(2)]
        par_in, u_in = m.sem("par_in"), [m.sem(f"u_in{i}") for i in range(2)]
        w_hi_done, w_lo_done, proj_done = m.sem("w_hi_d"), m.sem("w_lo_d"), m.sem("proj")
        sig_done, staged, stored = m.sem("sig"), m.sem("staged"), m.pool_dma_sem("stored")
        consts_done, par_act, par_dve = m.sem("consts"), m.sem("par_act"), m.sem("par_dve")
        chain = m.sem("chain")
        mats_done, ang_done, trig_done = m.sem("mats"), m.sem("ang"), m.sem("trig_d")
        xz_done, turned_done, msb_done, intra_in = m.sem("xz"), m.sem("turned"), m.sem("msb_d"), m.sem("intra_in")
        pin_done, hp_done, y_done, gelu_done = m.sem("pin_d"), m.sem("hp_d"), m.sem("y_d"), m.sem("gelu_d")
        last_y_out = m.sem("last_y_out")
        ys_out = [m.pool_dma_sem(f"ys_out{i}") for i in range(2)]
        zeroed = m.sem("zeroed")
        block = m.block()

        def slots(engine, body):
            for b in range(Z_BLOCKS):
                body(b, None, b % 2, b == 0, False)
            for p in range(2):
                body(Z_BLOCKS + p, p, p, p == 0, False)
            with engine.Fori(1, PAIRS // 2 - 1) as i:
                for r in range(2):
                    body(i * 2 + (Z_BLOCKS + r), i * 2 + r, r, False, False)
            for p in (PAIRS - 2, PAIRS - 1):
                body(Z_BLOCKS + p, p, p % 2, False, p == PAIRS - 1)

        @block.sync
        def _(sp):
            def load_weights(b, r):
                sp.dma_start(raw[:, r], a["w_in"][ds(b + UB, 1)].rearrange("a p k c -> (a p) k c")).then_inc(raw_in[r], 16)

            def load_u(p, r):
                for q in range(2):
                    src = a["us"][ds(p * 2 + q, 1)].rearrange("a c j n -> (a j) c n")
                    sp.dma_start(U[:, r, q], src).then_inc(u_in[r], 16)

            def body(b, p, r, first, last):
                if not (last or (p is not None and isinstance(p, int) and p == PAIRS - 2)):
                    sp.wait_ge(w_lo_done, b + 1)
                    load_weights(b + 2, r)
                if p is None:
                    if b == Z_BLOCKS - 1:
                        sp.wait_ge(stored, 16 * NT * U_BLOCKS)
                        load_u(0, 0)
                    return
                if not last:
                    if not first:
                        sp.wait_ge(y_done, p)
                    load_u(p + 1, 1 - r)
                sp.wait_ge(msb_done, p * 2 + 2)
                for j in range(SC):
                    rows = slice(j * GC, (j + 1) * GC)
                    sp.dma_start(w_intra[rows, r, :, j * GC:P], msb[:, :, 0:SC - j].rearrange("c q j d -> c q (j d)")
                                 ).then_inc(intra_in, 16)

            prefetched(sp, c, 1, raw_in)
            for dst, src in ((are[:], a["s5_a_re"]), (aim[:], a["s5_a_im"]), (bre[:], a["s5_b_re"]), (bim[:], a["s5_b_im"]),
                             (cre[:], a["s5_c_re"]), (cim[:], a["s5_c_im"]), (dd[:], a["s5_d"]),
                             (dt[0:NS], a["s5_log_dt"][0:1].to_broadcast([NS, PAIRS])),
                             (dt[NS:P], a["s5_log_dt"][1:2].to_broadcast([NS, PAIRS]))):
                sp.dma_start(dst, src).then_inc(par_in, 16)
            slots(sp, body)
            sp.wait_ge(w_lo_done, NB)
            prefetch(sp, c, [a["w_glu"][0:2], a["w_glu"][2:4]])
            sp.wait_ge(gelu_done, PAIRS)
            for q in range(2):
                sp.dma_start(a["ys"][GRP - 2 + q].rearrange("c j n -> j c n"), ysb[:, 1, q]).then_inc(last_y_out, 16)
            sp.wait_ge(last_y_out, 32)

        @block.gpsimd
        def _(pool):
            pool.iota(nn[:], pattern=[[1, NCK]], base=0, channel_multiplier=0,
                      allow_small_or_imprecise_dtypes=True).then_inc(consts_done, 1)
            pool.iota(kk[:, 0:SC + 1], pattern=[[1, SC + 1]], base=0, channel_multiplier=0,
                      allow_small_or_imprecise_dtypes=True).then_inc(consts_done, 1)
            pool.iota(kk[:, SC + 1:NL], pattern=[[-1, SC]], base=SC - 1, channel_multiplier=0,
                      allow_small_or_imprecise_dtypes=True).then_inc(consts_done, 1)
            pool.memset(w_intra[:], 0.0).then_inc(zeroed, 1)
            pool.memset(Hp[:], 0.0).then_inc(zeroed, 1)
            pool.wait_ge(zeroed, 2)

            def store_y(p, r):
                pool.wait_ge(gelu_done, p + 1)
                for q in range(2):
                    dst = a["ys"][ds(p * 2 + q, 1)].rearrange("a c j n -> (a j) c n")
                    pool.dma_start(dst, ysb[:, r, q]).then_inc(ys_out[r], 16)

            def body(b, p, r, first, last):
                if p is not None and not first:
                    store_y(p - 1, 1 - r)
                for t in range(NT):
                    pool.wait_ge(staged, b * NT + t + 1)
                    if p is None and b < U_BLOCKS:
                        dst = a["us"].rearrange("(k g) c j n -> k (g c) j n", k=S5KT)[b, :, :, t * NW:(t + 1) * NW]
                        src = stage[:, t].rearrange("p (j n) -> p j n", j=SC)
                    else:
                        out = a["silu_z"][b - U_BLOCKS:b - U_BLOCKS + 1] if p is None else a["gates"][ds(p, 1)]
                        dst = out[:, :, t * TT:(t + 1) * TT].rearrange("a p n -> (a p) n")
                        src = stage[:, t]
                    pool.dma_start(dst, src).then_inc(stored, 16)
                    pool.wait_ge(stored, (b * NT + t) * 16 + 16)
            slots(pool, body)
            for r in range(2):
                pool.wait_ge(ys_out[r], 16 * PAIRS - 32 * r)

        @block.tensor
        def _(pe):
            def project(b, r, t, first, ks=range(KT)):
                if not first and ks[0] == 0:
                    pe.wait_ge(staged, (b - 1) * NT + t + 1)
                at = slice(t * TT, (t + 1) * TT)
                for k in ks:
                    ins = split_matmuls(pe, ps[t][:], w_hi[:, r, k], w_lo[:, r, k], u_hi[:, k, at], u_lo[:, k, at],
                                        k == 0, k == KT - 1)
                if ks[-1] == KT - 1:
                    ins.then_inc(proj_done, 1)

            def body(b, p, r, first, last):
                pe.wait_ge(w_lo_done, b + 1)
                head = p is None and b == 0
                project(b, r, 0, head)
                project(b, r, 1, head, range(0, 3))
                if p is not None:
                    if not first:
                        pe.wait_ge(gelu_done, p)
                    pe.wait_ge(xz_done, p + 1)
                    for q in range(2):
                        pe.transpose(px[:, q * P:(q + 1) * P], X[:, q].rearrange("p j c -> p (j c)"), c["ident"][:])
                    for q in range(2):
                        rows = slice(q * NS, (q + 1) * NS)
                        for k in range(2):
                            ins = pe.matmul(py[q][0:GC, NCK:NCK + P], bb[rows, k],
                                            Z[rows, k, 0:SC].rearrange("p j c -> p (j c)"), start=k == 0, stop=k == 1)
                    ins.then_inc(mats_done, 1)
                project(b, r, 1, head, range(3, KT))
                project(b, r, 2, head, range(0, 2))
                if p is not None:
                    pe.wait_ge(turned_done, p + 1)
                    pe.wait_ge(u_in[r], (p // 2) * 32 + 32 if isinstance(p, int) else (p - r) * 16 + 32)
                    if not first:
                        pe.wait_ge(hp_done, p)
                    for k in range(2):
                        for q in range(2):
                            ins = pe.matmul(pin[q * NS:(q + 1) * NS, k * NCK:(k + 1) * NCK], w_in_t[:, k, q * NS:(q + 1) * NS],
                                            U[:, r, q], start=True, stop=True)
                    ins.then_inc(pin_done, 1)
                project(b, r, 2, head, range(2, KT))
                project(b, r, 3, head)
                if p is not None:
                    pe.wait_ge(intra_in, (p + 1) * 16 * SC)
                    pe.wait_ge(hp_done, p + 1)
                    for q in range(2):
                        pe.matmul(py[q][:, 0:NCK], w_intra[:, r, q], U[:, r, q], start=True, stop=False)
                    for k in range(2):
                        for q in range(2):
                            rows = slice(q * NS, (q + 1) * NS)
                            ins = pe.matmul(py[q][:, 0:NCK], Z[rows, k, 1:SC + 1].rearrange("p j c -> p (j c)"),
                                            Hp[rows, k], start=False, stop=k == 1)
                    ins.then_inc(y_done, 1)
            slots(pe, body)

        @block.scalar
        def _(act):
            n_par = [0]

            def par(ins):
                n_par[0] += 1
                ins.then_inc(par_act, 1)

            def round_weights(b, r):
                act.wait_ge(raw_in[r], (b // 2) * 16 + 16 if isinstance(b, int) else b * 8 - r * 8 + 16)
                act.activation(w_hi[:, r], raw[:, r], ACT.Copy).then_inc(w_hi_done, 1)

            def gelu(p, r):
                act.wait_ge(y_done, p + 1)
                if not (isinstance(p, int) and p < 2):
                    act.wait_ge(ys_out[r], (p - r) * 16)
                for q in range(2):
                    ins = act.activation(ysb[:, r, q], py[q][:, 0:NCK], ACT.Gelu_apprx_tanh)
                ins.then_inc(gelu_done, 1)

            def body(b, p, r, first, last):
                if p is not None:
                    if not first:
                        gelu(p - 1, 1 - r)
                    act.wait_ge(ang_done, p + 1)
                    act.activation(trig[:], trig[:], ACT.Sin, scale=TWO_PI).then_inc(trig_done, 1)
                    act.wait_ge(mats_done, p + 1)
                    act.activation(w_in_t[:].rearrange("p k n -> p (k n)"), px[:, 0:2 * P], ACT.Copy).then_inc(turned_done, 1)
                for t in range(NT):
                    act.wait_ge(proj_done, b * NT + t + 1)
                    if not (p is None and b == 0):
                        act.wait_ge(stored, ((b - 1) * NT + t) * 16 + 16)
                    if p is None and b < U_BLOCKS:
                        act.activation(stage[:, t].rearrange("p (j n) -> p j n", j=SC),
                                       ps[t][:].rearrange("p (n j) -> p j n", j=SC), ACT.Copy).then_inc(staged, 1)
                    elif p is None:
                        act.activation(stage[:, t], ps[t][:], ACT.Sigmoid).then_inc(sig_done, 1)
                    else:
                        act.activation(stage[:, t], ps[t][:], ACT.Sigmoid).then_inc(staged, 1)
                    if t == 0:
                        if not last:
                            round_weights(b + 1, 1 - r)

            round_weights(0, 0)
            act.wait_ge(par_in, 9 * 16)
            par(act.activation(dt[:], dt[:], ACT.Exp))
            act.wait_ge(par_dve, 4)
            par(act.activation(mag[:], mag[:], ACT.Exp))
            act.wait_ge(par_dve, 9)
            par(act.activation(li[:], li[:], ACT.Sin, scale=TWO_PI))
            par(act.activation(lr[:], lr[:], ACT.Sin, scale=TWO_PI))
            slots(act, body)
            gelu(PAIRS - 1, 1)

        @block.vector
        def _(dve):
            def split_weights(b, r):
                dve.wait_ge(w_hi_done, b + 1)
                dve.tensor_tensor(w_lo[:, r], raw[:, r], w_hi[:, r].bitcast(F32), ALU.subtract).then_inc(w_lo_done, 1)

            n_par = [0]

            def par(ins):
                n_par[0] += 1
                ins.then_inc(par_dve, 1)
                dve.wait_ge(par_dve, n_par[0])

            def parameters():
                bk = lambda x: x[:].rearrange("p (a b) -> p a b", b=1).to_broadcast([P, PAIRS, NL])
                bn = kk[:].rearrange("p (a b) -> p a b", a=1).to_broadcast([P, PAIRS, NL])
                at = lambda x, j: x[:, :, j:j + 1].rearrange("p a b -> p (a b)")
                dve.wait_ge(consts_done, 3)
                dve.wait_ge(par_act, 1)
                par(dve.tensor_tensor(adt[:], are[:], dt[:], ALU.mult))
                par(dve.scalar_tensor_tensor(turns[:], aim[:], 0.15915494309, dt[:], ALU.mult, ALU.mult))
                par(dve.tensor_tensor(tn[:], bk(turns), bn, ALU.mult))
                par(dve.tensor_tensor(mag[:], bk(adt), bn, ALU.mult))
                par(dve.tensor_scalar(li[:], tn[:], MAGIC, MAGIC, ALU.add, ALU.subtract))
                par(dve.tensor_tensor(tn[:], tn[:], li[:], ALU.subtract))
                par(dve.tensor_scalar(lr[:], tn[:], 0.25, None, ALU.add))
                par(dve.tensor_scalar(li[:], lr[:], MAGIC, MAGIC, ALU.add, ALU.subtract))
                dve.tensor_tensor(lr[:], lr[:], li[:], ALU.subtract).then_inc(chain, 1)
                dve.wait_ge(chain, 1)
                par(dve.tensor_copy(li[:], tn[:]))
                par(dve.tensor_scalar(f_hi[:], at(tn, SC), 192.0, 192.0, ALU.add, ALU.subtract))
                par(dve.tensor_tensor(f_lo[:], at(tn, SC), f_hi[:], ALU.subtract))
                dve.wait_ge(par_act, 4)
                par(dve.tensor_tensor(lr[:], lr[:], mag[:], ALU.mult))
                par(dve.tensor_tensor(li[:], li[:], mag[:], ALU.mult))
                par(dve.tensor_copy(rho[:], at(mag, SC)))
                par(dve.tensor_tensor(den[:], are[:], are[:], ALU.mult))
                par(dve.tensor_tensor(st[:], aim[:], aim[:], ALU.mult))
                par(dve.tensor_tensor(den[:], den[:], st[:], ALU.add))
                par(dve.reciprocal(den[:], den[:]))
                par(dve.tensor_scalar(nr[:], at(lr, 1), 1.0, None, ALU.subtract))
                par(dve.tensor_tensor(sr[:], nr[:], are[:], ALU.mult))
                par(dve.tensor_tensor(st[:], at(li, 1), aim[:], ALU.mult))
                par(dve.tensor_tensor(sr[:], sr[:], st[:], ALU.add))
                par(dve.tensor_tensor(sr[:], sr[:], den[:], ALU.mult))
                par(dve.tensor_tensor(si[:], at(li, 1), are[:], ALU.mult))
                par(dve.tensor_tensor(st[:], nr[:], aim[:], ALU.mult))
                par(dve.tensor_tensor(si[:], si[:], st[:], ALU.subtract))
                par(dve.tensor_tensor(si[:], si[:], den[:], ALU.mult))

            LINKS = 38

            def pair(p, r, first):
                n = [0]

                def link(ins):
                    n[0] += 1
                    ins.then_inc(chain, 1)
                    dve.wait_ge(chain, p * LINKS + (n[0] + 1))

                pc = ds(p, 1)
                power = lambda x, j0, nj: x[:, pc, j0:j0 + nj].rearrange("p a j -> p j a").to_broadcast([P, nj, GC])
                chan = lambda x, nj: x.to_broadcast([P, nj, GC])
                sin, cos = trig[:, 0], trig[:, 1]

                def matrices():
                    flat = lambda x: x[:, pc].rearrange("p a c -> p (a c)")
                    if not first:
                        dve.wait_ge(y_done, p)
                    link(dve.tensor_scalar(mt[:, 0], flat(bim), si[:, pc], None, ALU.mult))
                    link(dve.scalar_tensor_tensor(bb[:, 0], flat(bre), sr[:, pc], mt[:, 0], ALU.mult, ALU.subtract))
                    link(dve.tensor_scalar(mt[:, 0], flat(bim), sr[:, pc], None, ALU.mult))
                    link(dve.scalar_tensor_tensor(bb[:, 1], flat(bre), si[:, pc], mt[:, 0], ALU.mult, ALU.add))
                    rev = SC + 1
                    link(dve.tensor_tensor(X[:, 0], power(lr, rev, SC), chan(bb[:, 0:1], SC), ALU.mult))
                    link(dve.tensor_tensor(mt[:, 0:SC], power(li, rev, SC), chan(bb[:, 1:2], SC), ALU.mult))
                    link(dve.tensor_tensor(X[:, 0], X[:, 0], mt[:, 0:SC], ALU.subtract))
                    link(dve.tensor_tensor(X[:, 1], power(lr, rev, SC), chan(bb[:, 1:2], SC), ALU.mult))
                    link(dve.tensor_tensor(mt[:, 0:SC], power(li, rev, SC), chan(bb[:, 0:1], SC), ALU.mult))
                    link(dve.tensor_tensor(X[:, 1], X[:, 1], mt[:, 0:SC], ALU.add))
                    link(dve.tensor_tensor(Z[:, 0], power(lr, 0, SC + 1), chan(cre[:, pc], SC + 1), ALU.mult))
                    link(dve.tensor_tensor(mt[:], power(li, 0, SC + 1), chan(cim[:, pc], SC + 1), ALU.mult))
                    link(dve.tensor_tensor(Z[:, 0], Z[:, 0], mt[:], ALU.subtract))
                    link(dve.tensor_tensor(Z[:, 1], power(lr, 0, SC + 1), chan(cim[:, pc], SC + 1), ALU.mult))
                    link(dve.tensor_tensor(mt[:], power(li, 0, SC + 1), chan(cre[:, pc], SC + 1), ALU.mult))
                    link(dve.scalar_tensor_tensor(Z[:, 1].rearrange("p j c -> p (j c)"), Z[:, 1].rearrange("p j c -> p (j c)"),
                                                  -1.0, mt[:].rearrange("p j c -> p (j c)"), ALU.mult, ALU.subtract))
                    dve.sem_inc(xz_done, 1)

                def angles():
                    link(dve.tensor_scalar(t1[:], nn[:], f_hi[:, pc], None, ALU.mult))
                    link(dve.tensor_scalar(t2[:], t1[:], MAGIC, MAGIC, ALU.add, ALU.subtract))
                    link(dve.tensor_tensor(t1[:], t1[:], t2[:], ALU.subtract))
                    link(dve.scalar_tensor_tensor(t1[:], nn[:], f_lo[:, pc], t1[:], ALU.mult, ALU.add))
                    link(dve.tensor_scalar(t2[:], t1[:], MAGIC, MAGIC, ALU.add, ALU.subtract))
                    link(dve.tensor_tensor(sin, t1[:], t2[:], ALU.subtract))
                    link(dve.tensor_scalar(t1[:], sin, 0.25, None, ALU.add))
                    link(dve.tensor_scalar(t2[:], t1[:], MAGIC, MAGIC, ALU.add, ALU.subtract))
                    dve.tensor_tensor(cos, t1[:], t2[:], ALU.subtract).then_inc(ang_done, 1)

                def taps():
                    dve.wait_ge(mats_done, p + 1)
                    if not first:
                        dve.wait_ge(intra_in, p * 16 * SC)
                    for q in range(2):
                        src = py[q][0:GC, NCK:NCK + P]
                        dve.tensor_copy(msb[:, q, 1:SC].rearrange("c j d -> c (j d)"), src[:, GC:P])
                        dve.scalar_tensor_tensor(msb[:, q, 0], c["ident"][0:GC, 0:GC], dd[:, q, pc], src[:, 0:GC],
                                                 ALU.mult, ALU.add).then_inc(msb_done, 1)

                def states():
                    dve.wait_ge(trig_done, p + 1)
                    dve.wait_ge(pin_done, p + 1)
                    re, im = pin[:, 0:NCK], pin[:, NCK:2 * NCK]
                    link(dve.tensor_tensor(xt[:, 0], re, cos, ALU.mult))
                    link(dve.tensor_tensor(t1[:], im, sin, ALU.mult))
                    link(dve.tensor_tensor(xt[:, 0], xt[:, 0], t1[:], ALU.add))
                    link(dve.tensor_tensor(xt[:, 1], im, cos, ALU.mult))
                    link(dve.tensor_tensor(t2[:], re, sin, ALU.mult))
                    link(dve.tensor_tensor(xt[:, 1], xt[:, 1], t2[:], ALU.subtract))
                    for k in range(2):
                        link(dve.tensor_tensor_scan(xt[:, k], rho[:, pc].to_broadcast([P, NCK]), xt[:, k], 0.0, ALU.mult, ALU.add))
                    last = NCK - 1
                    link(dve.tensor_tensor(Hp[:, 0, 1:], xt[:, 0, 0:last], cos[:, 0:last], ALU.mult))
                    link(dve.tensor_tensor(t1[:, 0:last], xt[:, 1, 0:last], sin[:, 0:last], ALU.mult))
                    link(dve.tensor_tensor(Hp[:, 0, 1:], Hp[:, 0, 1:], t1[:, 0:last], ALU.subtract))
                    link(dve.tensor_tensor(Hp[:, 1, 1:], xt[:, 0, 0:last], sin[:, 0:last], ALU.mult))
                    link(dve.tensor_tensor(t2[:, 0:last], xt[:, 1, 0:last], cos[:, 0:last], ALU.mult))
                    link(dve.tensor_tensor(Hp[:, 1, 1:], Hp[:, 1, 1:], t2[:, 0:last], ALU.add))
                    assert n[0] == LINKS
                    dve.sem_inc(hp_done, 1)
                return matrices, angles, taps, states

            def body(b, p, r, first, last):
                if p is not None:
                    matrices, angles, taps, states = pair(p, r, first)
                    matrices()
                    angles()
                if p is None and b >= U_BLOCKS:
                    for t in range(NT):
                        e = b * NT + t
                        dve.wait_ge(sig_done, e - U_BLOCKS * NT + 1)
                        dve.tensor_tensor(stage[:, t], ps[t][:], stage[:, t], ALU.mult).then_inc(staged, 1)
                        if t == 0:
                            split_weights(b + 1, 1 - r)
                elif not last:
                    split_weights(b + 1, 1 - r)
                if p is not None:
                    taps()
                    states()

            split_weights(0, 0)
            parameters()
            dve.wait_ge(zeroed, 2)
            slots(dve, body)


class Tile:

    def __init__(self, bank, use):
        self.bank, self.use = bank, use


def phase_tail(nc, c, a):
    BANKS = 6
    KTS = dict(glu=S5KT, os5=S5KT, ple=PLEKT, ohg=KT, out=KT, pgate=KT)
    PRO = ["glu", "os5"]
    BODY = ["ohg", "out", "glu", "ple", "pgate", "os5"]
    LAST = ["ohg", "out", "ple", "pgate"]
    units_of = lambda s: KTS[s]
    UPRO, UBODY = sum(map(units_of, PRO)), sum(map(units_of, BODY))
    TPRO, TBODY = 8 * len(PRO), 8 * len(BODY)
    assert UPRO % 2 == 0 and UBODY % 2 == 0 and TBODY % BANKS == 0
    R_BODY = dict(ohg=0, glu=8, pgate=12)

    with Bufs(nc, "t") as m:
        two = lambda n, kt: [m.sb(f"{n}_{x}", [P, kt, TT], F32R) for x in ("hi", "lo")]
        acts_a, acts_b = two("oa", KT), two("mb", KT)
        acts_y, acts_z, acts_p = two("ya", S5KT), two("za", S5KT), two("pa", PLEKT)
        acts = dict(glu=acts_y, os5=acts_z, ple=acts_p, ohg=acts_a, out=acts_b, pgate=acts_a)
        h = m.sb("h", [P, KT, TT])
        mp = m.sb("mp", [P, KT, TT])
        raw = c["raw"][:].rearrange("p a k c -> p a (k c)")
        w_hi = m.sb("w_hi", [P, 2, KT * P], F32R)
        w_lo = m.sb("w_lo", [P, 2, KT * P], F32R)
        ein = m.sb("ein", [P, 4, TT])
        xa = m.sb("xa", [P, 2, TT])
        xn = m.sb("xn", [P, 2, TT])
        r = m.sb("r", [P, 2, TT])
        sgb = m.sb("sgb", [P, 2, TT])
        sq, sumsq = m.sb("sq", [P, TT]), m.sb("sumsq", [P, TT])
        rstd = m.sb("rstd", [P, 2, TT])
        ps = [m.ps(f"ps{i}") for i in range(BANKS)]
        ms = [m.ps(f"ms{i}") for i in range(2)]
        filled = [m.sem(f"filled{i}") for i in range(BANKS)]
        drained = [m.sem(f"drained{i}") for i in range(BANKS)]
        raw_in = [m.sem(f"raw_in{i}") for i in range(2)]
        ein_in = [m.sem(f"ein_in{i}") for i in range(4)]
        xa_in = [m.pool_dma_sem(f"xa_in{i}") for i in range(2)]
        first_xa_in = [m.sem(f"first_xa_in{i}") for i in range(S5KT)]
        h_in, stored = m.pool_dma_sem("h_in"), m.pool_dma_sem("stored")
        last_stored = m.sem("last_stored")
        w_hi_done, w_lo_done = m.sem("w_hi_d"), m.sem("w_lo_d")
        x_hi_done, x_lo_done = m.sem("x_hi"), m.sem("x_lo")
        r_set, r_hi_done, r_done = m.sem("r_set"), m.sem("r_hi"), m.sem("r_done")
        pool_waits = m.sem("pool_waits")
        glu_half = m.sem("glu_half")
        sq_done, summed = m.sem("sq_d"), m.sem("summed")
        ms_done, ln_done, rstd_done = m.sem("ms_d"), m.sem("ln_d"), m.sem("rstd_d")
        n_set, n_hi_done, n_lo_done, fin_done = m.sem("n_set"), m.sem("n_hi"), m.sem("n_lo"), m.sem("fin")
        block = m.block()

        def tile(sec, t, j, body):
            order = PRO if not body else (LAST if isinstance(t, int) and t == NT - 1 else BODY)
            at = 8 * order.index(sec) + j
            if not body:
                return Tile(at % BANKS, at // BANKS)
            return Tile((TPRO + at) % BANKS, t * (TBODY // BANKS) + (TPRO + at) // BANKS)

        def run(engine, unit):
            def iteration(t, secs, base, body, first, last):
                n = 0
                for sec in secs:
                    for i in range(units_of(sec)):
                        unit(sec, t, body, base + n, i, first, last)
                        n += 1
            iteration(0, PRO, 0, False, True, False)
            iteration(0, BODY, UPRO, True, True, False)
            with engine.Fori(1, NT - 1) as t:
                iteration(t, BODY, t * UBODY + UPRO, True, False, False)
            iteration(NT - 1, LAST, (NT - 1) * UBODY + UPRO, True, False, True)

        def parity(sec, body, t, i):
            order = PRO if not body else (LAST if isinstance(t, int) and t == NT - 1 else BODY)
            return (sum(units_of(s) for s in order[:order.index(sec)]) + i) % 2

        def following(sec, body, t, i, by):
            its = lambda order, t, body: [(s, k, t + 1 if body and s in PRO else t) for s in order for k in range(units_of(s))]
            last = isinstance(t, int) and t == NT - 1
            seq = its(PRO if not body else LAST if last else BODY, t, body)
            nxt = [] if last and body else its(LAST if isinstance(t, int) and t == NT - 2 and body else BODY, t + 1 if body else 0, True)
            at = [k for k, x in enumerate(seq) if x[0] == sec and x[1] == i][0]
            both = seq + nxt
            return both[at + by] if at + by < len(both) else None

        def r_index(sec, t, body, j):
            if sec == "pgate" and isinstance(t, int) and t == NT - 1:
                return t * 20 + (4 + 8 + j)
            return j if not body else t * 20 + (4 + R_BODY[sec] + j)

        def slot(sec, body, j, what):
            if what == "r":
                return (j if not body else R_BODY[sec] + j) % 2
            return ((dict(glu=0, os5=4)[sec] if not body else dict(ohg=0, glu=8, os5=12)[sec]) + j) % 4

        def ein_ready(engine, sec, t, body, j):
            at = dict(glu=0, os5=4)[sec] + j if not body else 12 + dict(ohg=0, glu=8, os5=12)[sec] + j
            n = at // 4 + 1
            engine.wait_ge(ein_in[slot(sec, body, j, "e")], n * 16 if not body else t * 80 + n * 16)

        def loads_after(sec, t, body, i):
            order = PRO if not body else (LAST if isinstance(t, int) and t == NT - 1 else BODY)
            at = sum(units_of(s) for s in order[:order.index(sec)]) + i + (UPRO if body else 0)
            n = (at // 2 + 2) * 16
            return t * (UBODY // 2 * 16) + n if body else n

        def x_buffer(body, what, k, half):
            return (xn if not body and what == "y" and k >= 2 else xa)[:, half]

        def y_source(k, t):
            return a["ys"].rearrange("(k g) c j n -> k (g c) j n", k=S5KT)[k, :, :, ds(t * (TT // SC), TT // SC)]

        @block.sync
        def _(sp):
            weights = dict(glu="w_glu", os5="w_o_s5", ple="w_ple", ohg="w_o_hg", out="w_out", pgate="w_ple_gate")

            def load_weights(sec, i, half):
                n = KT // KTS[sec]
                sp.dma_start(raw[:, half].rearrange("p (b k c) -> p b k c", b=n, c=P),
                             a[weights[sec]][i * n:(i + 1) * n].rearrange("b p k c -> p b k c")).then_inc(raw_in[half], 16)

            def load_ein(sec, i, t_data):
                src, js = {"glu": (a["silu_z"], [i]), "os5": (a["gates"][KT:2 * KT], [2 * i, 2 * i + 1]),
                           "ohg": (a["gates"][0:KT], [i])}.get(sec, (None, []))
                for j in js:
                    body = not (sec in PRO and isinstance(t_data, int) and t_data == 0)
                    t = t_data - 1 if sec in PRO and body else t_data
                    for sem, value in uses(sec, t, body, j):
                        sp.wait_ge(sem, value)
                    quarter = slot(sec, body, j, "e")
                    sp.dma_start(ein[:, quarter], src[j, :, ds(t_data * TT, TT)]).then_inc(ein_in[quarter], 16)

            def uses(sec, t, body, j):
                pro = [("glu", k) for k in range(4)] + [("os5", k) for k in range(8)]
                bod = [("ohg", k) for k in range(8)] + [("glu", k) for k in range(4)] + [("os5", k) for k in range(8)]
                at = (pro if not body else bod).index((sec, j))
                if at >= 4:
                    s, k, tt, bd = *(pro if not body else bod)[at - 4], t, body
                elif not body:
                    return []
                elif isinstance(t, int) and t == 0:
                    s, k, tt, bd = *pro[at + 8], 0, False
                else:
                    s, k, tt, bd = *bod[at + 16], t - 1, True
                if s == "glu":
                    return [(r_set, r_index("glu", tt, bd, k) + 1)]
                x = tile(s, tt, k, bd)
                return [(drained[x.bank], x.use + 1)]

            def unit(sec, t, body, u, i, first, last):
                nxt = following(sec, body, t, i, 1)
                if nxt:
                    load_ein(*nxt)
                nxt = following(sec, body, t, i, 2)
                if nxt:
                    sp.wait_ge(w_lo_done, u + 1)
                    load_weights(nxt[0], nxt[1], parity(sec, body, t, i))

            for k in range(S5KT):
                sp.dma_start((xa if k < 2 else xn)[:, k % 2], y_source(k, 0)).then_inc(first_xa_in[k], 16)
            prefetched(sp, c, 2, raw_in)
            load_ein("glu", 0, 0)
            run(sp, unit)
            for k in range(KT):
                sp.wait_ge(fin_done, (NT - 1) * KT + k + 1)
                sp.dma_start(a["out"][k, :, (NT - 1) * TT:], h[:, k]).then_inc(last_stored, 16)
            sp.wait_ge(last_stored, 16 * KT)

        XPRO = [("y", k) for k in range(S5KT)] + [("o", k) for k in range(KT)]
        XBODY = [("p", k) for k in range(PLEKT)] + XPRO

        @block.gpsimd
        def _(pool):
            def load_xa(n, half, what, k, t):
                pool.wait_ge(x_lo_done, n - 1)
                pool.sem_inc(pool_waits, 1)
                if what == "y":
                    src = y_source(k, t)
                elif what == "o":
                    src = a["o_gated"][k, :, ds(t * TT, TT)]
                else:
                    src = a["p"][:, k, ds(t * TT, TT)]
                pool.dma_start(xa[:, half], src).then_inc(xa_in[half], 16)

            def load_h(t):
                pool.dma_start(h[:], a["x"][:, :, ds(t * TT, TT)]).then_inc(h_in, 16)

            def store(t):
                for k in range(KT):
                    pool.wait_ge(fin_done, t * KT + k + 1)
                    pool.sem_inc(pool_waits, 1)
                    pool.dma_start(a["out"][k, :, ds(t * TT, TT)], h[:, k]).then_inc(stored, 16)
                pool.wait_ge(stored, t * (16 * KT) + 16 * KT)
                pool.sem_inc(pool_waits, 1)

            def iteration(t, first, last):
                for n, (what, k) in enumerate(XBODY):
                    if n == PLEKT + 2 and not first:
                        store(t - 1)
                        load_h(t)
                    if what == "p" or not last:
                        load_xa(t * len(XBODY) + (len(XPRO) + n), n % 2, what, k, t if what == "p" else t + 1)
            for n, (what, k) in enumerate(XPRO):
                if what == "o":
                    load_xa(n, n % 2, what, k, 0)
                if n == len(XPRO) - 3:
                    load_h(0)
            iteration(0, True, False)
            with pool.Fori(1, NT - 1) as t:
                iteration(t, False, False)
            iteration(NT - 1, False, True)

        def x_number(t, body, what, k):
            at = XPRO.index((what, k)) if not body else len(XPRO) + XBODY.index((what, k))
            if not body:
                return at, at % 2, at // 2 - S5KT // 2 + 1
            return t * len(XBODY) + at, at % 2, t * (len(XBODY) // 2) + (at // 2 - S5KT // 2 + 1)

        def x_splits(sec, i, body, first, last):
            if not body:
                return [("o", 2 * i), ("o", 2 * i + 1)] if sec == "glu" else []
            if sec == "ohg":
                return [("p", i)] if i < PLEKT else [("y", i - 4)] if i >= 4 and not last else []
            return [("o", 2 * i), ("o", 2 * i + 1)] if sec == "os5" else []

        def finals(sec, i, body, first):
            return [2 * i, 2 * i + 1] if body and sec == "ohg" and not first and i < KT // 2 else []

        def norms(sec, i, body, last):
            if not body:
                return []
            if last:
                return {("ple", 0): [0, 1, 2, 3], ("ple", 1): [4, 5, 6, 7]}.get((sec, i), [])
            return {("glu", 1): [0, 1], ("glu", 2): [2, 3], ("glu", 3): [4, 5], ("ple", 0): [6], ("ple", 1): [7]}.get((sec, i), [])

        @block.tensor
        def _(pe):
            def mean_square(which, t, use):
                pe.wait_ge(summed, t * 16 + 8 * which + 8)
                if use is not None:
                    pe.wait_ge(ln_done, use)
                pe.matmul(ms[which][:], c["ones"][:], sumsq[:], start=True, stop=True).then_inc(ms_done, 1)

            def unit(sec, t, body, u, i, first, last):
                pe.wait_ge(w_lo_done, u + 1)
                kt, half = KTS[sec], parity(sec, body, t, i)

                def input_ready(k):
                    if sec == "ohg":
                        pe.wait_ge(x_lo_done, x_number(t - 1, not first, "o", k)[0] + 1)
                    elif sec == "out":
                        pe.wait_ge(r_done, r_index("ohg", t, body, k) + 1)
                    elif sec == "os5":
                        pe.wait_ge(r_done, r_index("glu", t, body, k) + 1)
                    elif sec == "pgate":
                        pe.wait_ge(n_lo_done, t * KT + (k + 1))
                    else:
                        pe.wait_ge(x_lo_done, x_number(t, body, "y" if sec == "glu" else "p", k)[0] + 1)

                hi, lo = acts[sec]
                for bl in range(KT // kt):
                    j = i * (KT // kt) + bl
                    x = tile(sec, t, j, body)
                    if not (isinstance(x.use, int) and x.use == 0):
                        pe.wait_ge(drained[x.bank], x.use)
                    for k in range(kt):
                        if i == 0 and bl == 0:
                            input_ready(k)
                        at = slice((bl * kt + k) * P, (bl * kt + k + 1) * P)
                        ins = split_matmuls(pe, ps[x.bank][:], w_hi[:, half, at], w_lo[:, half, at], hi[:, k], lo[:, k],
                                            k == 0, k == kt - 1)
                    ins.then_inc(filled[x.bank], 1)
                if body and sec == ("ple" if last else "glu") and i == 0:
                    mean_square(0, t, None if first else t * 2)
                if body and not last and sec == "os5" and i == 0:
                    mean_square(1, t, None if first else t * 2)

            run(pe, unit)
            mean_square(1, NT - 1, 2 * NT - 1)

        @block.scalar
        def _(act):
            def round_weights(half, loads):
                act.wait_ge(raw_in[half], loads)
                act.activation(w_hi[:, half], raw[:, half], ACT.Copy).then_inc(w_hi_done, 1)

            def one_over_rms(which, t, preload=True):
                if preload:
                    act.preload_act_table_set("natural_log_exp_and_others")
                if which and not (isinstance(t, int) and t == 0):
                    act.wait_ge(fin_done, t * KT)
                act.wait_ge(ms_done, t * 2 + which + 1)
                act.activation(rstd[:, which], ms[which][:], ACT.Ln, scale=1.0 / D, bias=c["eps"][:]).then_inc(ln_done, 1)
                act.wait_ge(ln_done, t * 2 + which + 1)
                act.activation(rstd[:, which], rstd[:, which], ACT.Exp, scale=-0.5).then_inc(rstd_done, 1)

            def square(number, k):
                if not (isinstance(number, int) and number == 0):
                    act.wait_ge(summed, number)
                act.activation(sq[:], h[:, k], ACT.Square).then_inc(sq_done, 1)

            def round_r(sec, t, body, j):
                n, half = r_index(sec, t, body, j), slot(sec, body, j, "r")
                act.wait_ge(r_set, n + 1)
                act.activation((acts_z if sec == "glu" else acts_b)[0][:, j], r[:, half], ACT.Copy).then_inc(r_hi_done, 1)

            def round_x(t, body, what, k):
                n, half, loads = x_number(t, body, what, k)
                if not body and what == "y":
                    act.wait_ge(first_xa_in[k], 16)
                else:
                    act.wait_ge(xa_in[half], loads * 16)
                src, dst = x_buffer(body, what, k, half), dict(y=acts_y, o=acts_a, p=acts_p)[what][0][:, k]
                if what == "y":
                    src = src.rearrange("p (j n) -> p n j", j=SC)
                    dst = dst.rearrange("p (n j) -> p n j", j=SC)
                act.activation(dst, src, ACT.Copy).then_inc(x_hi_done, 1)

            def unit(sec, t, body, u, i, first, last):
                blocks = KT // KTS[sec]
                for bl in range(blocks):
                    j = i * blocks + bl
                    x = tile(sec, t, j, body)
                    if sec == "glu" and bl == 0:
                        act.wait_ge(filled[x.bank], x.use + 1)
                        if body or i >= 2:
                            act.wait_ge(glu_half, (t * 4 + (4 + i - 1)) if body else i - 1)
                        at = KT // 2 + i
                        act.activation(sgb[:, i % 2], ps[x.bank][:], ACT.Sigmoid, bias=c["b_glu"][:, at:at + 1]
                                       ).then_inc(drained[x.bank], 1)
                    elif sec == "glu":
                        round_r(sec, t, body, i)
                    elif sec == "ohg":
                        round_r(sec, t, body, j)
                    elif sec == "ple":
                        act.wait_ge(filled[x.bank], x.use + 1)
                        if j == 0:
                            act.wait_ge(r_set, r_index("ohg", t, body, 7) + 1)
                        act.activation(mp[:, j], ps[x.bank][:], ACT.Copy).then_inc(drained[x.bank], 1)
                    elif sec == "out":
                        if last and j == KT - 1:
                            act.preload_act_table_set("natural_log_exp_and_others")
                        act.wait_ge(drained[x.bank], x.use + 1)
                        square(t * 16 + j, j)
                    elif sec == "pgate":
                        act.wait_ge(filled[x.bank], x.use + 1)
                        n, half = r_index(sec, t, body, j), slot(sec, body, j, "r")
                        act.wait_ge(r_done, n - 1)
                        act.activation(r[:, half], ps[x.bank][:], ACT.Sigmoid).then_inc(drained[x.bank], 1)
                        if last and j == KT - 1:
                            act.preload_act_table_set("natural_log_exp_and_others")
                        act.wait_ge(r_done, n + 1)
                        square(t * 16 + 8 + j, j)
                if following(sec, body, t, i, 2):
                    act.wait_ge(filled[x.bank], x.use + 1)
                    round_weights(parity(sec, body, t, i), loads_after(sec, t, body, i))
                if body and sec == ("ple" if last else "glu") and i == 0:
                    one_over_rms(0, t, not last)
                if body and sec == "os5" and i == 0:
                    one_over_rms(1, t)
                for k in norms(sec, i, body, last):
                    act.wait_ge(n_set, t * KT + k + 1)
                    act.activation(acts_a[0][:, k], xn[:, k % 2], ACT.Copy).then_inc(n_hi_done, 1)
                for what, k in x_splits(sec, i, body, first, last):
                    round_x(t, body, what, k)

            round_weights(0, 16)
            for k in range(S5KT):
                round_x(0, False, "y", k)
            round_weights(1, 16)
            run(act, unit)
            one_over_rms(1, NT - 1, False)

        @block.vector
        def _(dve):
            def split_weights(number, half):
                dve.wait_ge(w_hi_done, number + 1)
                dve.tensor_tensor(w_lo[:, half], raw[:, half], w_hi[:, half].bitcast(F32), ALU.subtract).then_inc(w_lo_done, 1)

            def hi_number(sec, t, body, j):
                return j if not body else t * 12 + (4 + (0 if sec == "ohg" else 8) + j)

            def split_r(sec, t, body, j):
                half, buf = slot(sec, body, j, "r"), acts_z if sec == "glu" else acts_b
                dve.wait_ge(r_hi_done, hi_number(sec, t, body, j) + 1)
                dve.tensor_tensor(buf[1][:, j], r[:, half], buf[0][:, j].bitcast(F32), ALU.subtract).then_inc(r_done, 1)

            def add_square(number, start, sums):
                dve.wait_ge(sq_done, number + 1)
                if start:
                    if not (isinstance(number, int) and number == 0):
                        dve.wait_ge(ms_done, sums)
                    dve.tensor_copy(sumsq[:], sq[:]).then_inc(summed, 1)
                else:
                    dve.wait_ge(summed, number)
                    dve.tensor_tensor(sumsq[:], sumsq[:], sq[:], ALU.add).then_inc(summed, 1)

            def norm(t, k):
                if k == 0:
                    dve.wait_ge(rstd_done, t * 2 + 1)
                if not (isinstance(t, int) and t == 0 and k < 2):
                    dve.wait_ge(n_lo_done, t * KT + k - 1)
                dve.scalar_tensor_tensor(xn[:, k % 2], h[:, k], c["ple_g"][:, k:k + 1], rstd[:, 0], ALU.mult, ALU.mult
                                         ).then_inc(n_set, 1)

            def split_norm(t, k):
                dve.wait_ge(n_hi_done, t * KT + k + 1)
                dve.tensor_tensor(acts_a[1][:, k], xn[:, k % 2], acts_a[0][:, k].bitcast(F32), ALU.subtract).then_inc(n_lo_done, 1)

            def unit(sec, t, body, u, i, first, last):
                normed = norms(sec, i, body, last)

                def while_rounded():
                    for k in normed[:2]:
                        norm(t, k)
                    for k in finals(sec, i, body, first):
                        final(t - 1, k)

                if sec == "ple":
                    while_rounded()
                blocks = KT // KTS[sec]
                for bl in range(blocks):
                    j = i * blocks + bl
                    x = tile(sec, t, j, body)
                    p_ = ps[x.bank][:]
                    if sec == "glu" and bl == 1:
                        n, half = r_index(sec, t, body, i), slot(sec, body, i, "r")
                        gate = tile(sec, t, j - 1, body)
                        if body or i >= 2:
                            dve.wait_ge(r_done, n - 1)
                        dve.wait_ge(drained[gate.bank], gate.use + 1)
                        dve.wait_ge(filled[x.bank], x.use + 1)
                        dve.scalar_tensor_tensor(r[:, half], p_, c["b_glu"][:, i:i + 1], sgb[:, i % 2], ALU.add, ALU.mult
                                                 ).then_inc(drained[x.bank], 1)
                        dve.wait_ge(drained[x.bank], x.use + 1)
                        dve.sem_inc(glu_half, 1)
                        ein_ready(dve, sec, t, body, i)
                        dve.tensor_tensor(r[:, half], r[:, half], ein[:, slot(sec, body, i, "e")], ALU.mult).then_inc(r_set, 1)
                        while_rounded()
                        split_r(sec, t, body, i)
                    elif sec == "os5":
                        ein_ready(dve, sec, t, body, j)
                        dve.wait_ge(filled[x.bank], x.use + 1)
                        dve.tensor_tensor(mp[:, j], p_, ein[:, slot(sec, body, j, "e")], ALU.mult).then_inc(drained[x.bank], 1)
                    elif sec == "ohg":
                        n, half = r_index(sec, t, body, j), slot(sec, body, j, "r")
                        dve.wait_ge(r_done, n - 1)
                        ein_ready(dve, sec, t, body, j)
                        dve.wait_ge(filled[x.bank], x.use + 1)
                        dve.tensor_tensor(r[:, half], p_, ein[:, slot(sec, body, j, "e")], ALU.mult).then_inc(drained[x.bank], 1)
                        dve.wait_ge(drained[x.bank], x.use + 1)
                        dve.tensor_tensor(r[:, half], r[:, half], mp[:, j], ALU.add).then_inc(r_set, 1)
                        while_rounded()
                        split_r(sec, t, body, j)
                    elif sec == "out":
                        if j == 0:
                            dve.wait_ge(h_in, t * 16 + 16)
                        dve.wait_ge(filled[x.bank], x.use + 1)
                        dve.tensor_tensor(h[:, j], p_, h[:, j], ALU.add).then_inc(drained[x.bank], 1)
                        add_square(t * 16 + j, j == 0, t * 2)
                    elif sec == "pgate":
                        n, half = r_index(sec, t, body, j), slot(sec, body, j, "r")
                        dve.wait_ge(drained[x.bank], x.use + 1)
                        dve.tensor_tensor(r[:, half], r[:, half], mp[:, j], ALU.mult).then_inc(r_set, 1)
                        dve.wait_ge(r_set, n + 1)
                        dve.tensor_tensor(h[:, j], h[:, j], r[:, half], ALU.add).then_inc(r_done, 1)
                        add_square(t * 16 + 8 + j, j == 0, t * 2 + 1)
                if following(sec, body, t, i, 2):
                    split_weights(u + 2, parity(sec, body, t, i))
                for k in normed:
                    split_norm(t, k)
                    if k + 2 in normed:
                        norm(t, k + 2)
                for what, k in x_splits(sec, i, body, first, last):
                    split_x(t, body, what, k)

            def split_x(t, body, what, k):
                n, half, loads = x_number(t, body, what, k)
                dve.wait_ge(x_hi_done, n + 1)
                hi, lo = (x[:, k] for x in dict(y=acts_y, o=acts_a, p=acts_p)[what])
                src, hi = x_buffer(body, what, k, half), hi.bitcast(F32)
                if what == "y":
                    src = src.rearrange("p (j n) -> p n j", j=SC)
                    hi, lo = (x.rearrange("p (n j) -> p n j", j=SC) for x in (hi, lo))
                dve.tensor_tensor(lo, src, hi, ALU.subtract).then_inc(x_lo_done, 1)

            def final(t, k):
                if k == 0:
                    dve.wait_ge(rstd_done, t * 2 + 2)
                dve.scalar_tensor_tensor(h[:, k], h[:, k], c["fin_g"][:, k:k + 1], rstd[:, 1], ALU.mult, ALU.mult
                                         ).then_inc(fin_done, 1)

            split_weights(0, 0)
            for k in range(S5KT):
                split_x(0, False, "y", k)
            split_weights(1, 1)
            run(dve, unit)
            for k in range(KT):
                final(NT - 1, k)


def build(nc, a):
    with ExitStack() as keep, Bufs(nc, "c") as m:
        Bufs.keep = keep
        c = dict(norm_g=m.sb("norm_g", [P, KT]), ple_g=m.sb("ple_g", [P, KT]), fin_g=m.sb("fin_g", [P, KT]),
                 hg_g=m.sb("hg_g", [P, HEADS]), b_glu=m.sb("b_glu", [P, KT]), lb=m.sb("lb", [P, HEADS]),
                 omlb=m.sb("omlb", [P, HEADS]), nomlb=m.sb("nomlb", [P, HEADS]), eps=m.sb("eps", [P, 1]),
                 ones=m.sb("ones", [P, P]), ident=m.sb("ident", [P, P]), causal=m.sb("causal", [P, P]),
                 restart=m.sb("restart", [P, TT]), raw=m.sb("raw", [P, 2, KT, P]),
                 prefetched=[m.sem(f"prefetched{i}") for i in range(2)])
        with Bufs(nc, "u") as mu:
            u_hi = mu.sb("hi", [P, KT, SEQ], F32R)
            u_lo = mu.sb("lo", [P, KT, SEQ], F32R)
            phase_norm_in(nc, c, a, u_hi, u_lo)
            phase_hgrn(nc, c, a, u_hi, u_lo)
            phase_s5(nc, c, a, u_hi, u_lo)
        phase_tail(nc, c, a)


SCRATCH = dict(o_gated=(HEADS, P, SEQ), us=(GRP, GC, SC, NCK), ys=(GRP, GC, SC, NCK), silu_z=(S5KT, P, SEQ),
               gates=(2 * KT, P, SEQ))


def columns(v):
    return v.reshape(-1, P).T


def weight_blocks(w):
    k, n = w.shape
    return w.reshape(k // P, P, n // P, P).transpose(2, 1, 0, 3)


def time_last(v):
    return v.T.reshape(-1, P, v.shape[0]).transpose(1, 0, 2)


def state_pairs(v):
    v = v.reshape((PAIRS, 2, NS) + v.shape[2:])
    return v.transpose((1, 2, 0) + tuple(range(3, v.ndim))).reshape((P, PAIRS) + v.shape[3:])


def kernel(x, p, norm_g, w_in, hg_lb, hg_norm_g, w_o_hg, s5_a_re, s5_a_im, s5_log_dt, s5_b_re, s5_b_im, s5_c_re, s5_c_im,
           s5_d, w_glu, b_glu, w_o_s5, w_out, ple_norm_g, w_ple, w_ple_gate, final_norm_g):
    import numpy as np
    import concourse.bacc as bacc
    from concourse.bass_utils import run_bass_kernel_spmd

    glu = weight_blocks(w_glu[0])
    half = glu.shape[0] // 2
    laid_out = dict(
        x=time_last(x[0]), p=time_last(p[0, 0]), norm_g=columns(norm_g[0]), w_in=weight_blocks(w_in[0]),
        hg_lb=hg_lb.reshape(2, HEADS, P).transpose(2, 0, 1), hg_norm_g=columns(hg_norm_g[0]), w_o_hg=weight_blocks(w_o_hg[0]),
        s5_a_re=state_pairs(s5_a_re[0]), s5_a_im=state_pairs(s5_a_im[0]), s5_log_dt=s5_log_dt[0].reshape(PAIRS, 2).T,
        s5_b_re=state_pairs(s5_b_re[0]), s5_b_im=state_pairs(s5_b_im[0]),
        s5_c_re=state_pairs(s5_c_re[0].transpose(0, 2, 1)), s5_c_im=state_pairs(s5_c_im[0].transpose(0, 2, 1)),
        s5_d=s5_d[0].reshape(PAIRS, 2, GC).transpose(2, 1, 0),
        w_glu=np.stack([glu[half:], glu[:half]], axis=1).reshape(glu.shape), b_glu=columns(b_glu[0]),
        w_o_s5=weight_blocks(w_o_s5[0]), w_out=weight_blocks(w_out[0]), ple_norm_g=columns(ple_norm_g[0]),
        w_ple=weight_blocks(w_ple[0]), w_ple_gate=weight_blocks(w_ple_gate[0]), final_norm_g=columns(final_norm_g))
    nc = bacc.Bacc("TRN2", target_bir_lowering=False, num_devices=1)
    arrays, dram = {}, {}
    for name, v in laid_out.items():
        arrays[f"{name}_in"] = np.ascontiguousarray(v)
        dram[name] = nc.dram_tensor(f"{name}_in", v.shape, F32, kind="ExternalInput").ap()
    for name, shape in SCRATCH.items():
        dram[name] = nc.dram_tensor(f"{name}_scratch", shape, F32, kind="Internal").ap()
    dram["out"] = nc.dram_tensor("out_t", (KT, P, SEQ), F32, kind="ExternalOutput").ap()
    build(nc, dram)
    result = run_bass_kernel_spmd(nc, [arrays], core_ids=[0]).results[0]["out_t"]
    return np.ascontiguousarray(result.reshape(D, SEQ).T).reshape(x.shape)
```
